# Optimizing a Trainium2 kernel written in Bass

```python
import jax, jax.numpy as jnp
from jax import lax
import numpy as np

D_MODEL = 1024
BATCH = 1
SEQ = 256
DEPTH = 2

CHUNK = 64
N_MIXERS = 2
HG_HEADS = 8
HG_KEY = 128
HG_VAL = D_MODEL // HG_HEADS
HG_KEY_TOT = HG_HEADS * HG_KEY
SW_Q_HEADS = 16
SW_KV_HEADS = 4
SW_HEAD_DIM = D_MODEL // SW_Q_HEADS
SW_GROUP = SW_Q_HEADS // SW_KV_HEADS
WINDOW = 128
WINDOW_CHUNKS = WINDOW // CHUNK
ROPE_THETA = 500000.0
ROPE_DIM = SW_HEAD_DIM // 4
D_FF = 2816
FFN_RES_WEIGHT = 0.5
NORM_EPS = 1e-6
N_ADA = 9
N_HGRN = (DEPTH + 1) // 2
N_SWA = DEPTH // 2

kernel_name = "hybrid_hgrn2_swa_sink_macaron_adaln"

def rms_norm(x, g):
    xf = x.astype(jnp.float32)
    y = xf * lax.rsqrt(jnp.mean(xf * xf, axis=-1, keepdims=True) + NORM_EPS)
    return (y * g.astype(jnp.float32)).astype(x.dtype)

def modulate(h, shift, scale):
    return h * (1 + scale[:, None, :]) + shift[:, None, :]

def swiglu_ffn(h, w_gu, w_down):
    gate, up = jnp.split(h @ w_gu, 2, axis=-1)
    return (jax.nn.silu(gate) * up) @ w_down

def partial_rotary(x, positions):
    half = ROPE_DIM // 2
    inv_freq = ROPE_THETA ** (-jnp.arange(half, dtype=jnp.float32) / half)
    ang = positions.astype(jnp.float32)[..., None] * inv_freq
    cos = jnp.cos(ang)[:, :, None, :]
    sin = jnp.sin(ang)[:, :, None, :]
    xr = x[..., :ROPE_DIM].astype(jnp.float32)
    x1, x2 = xr[..., :half], xr[..., half:]
    rot = jnp.concatenate([x1 * cos - x2 * sin, x2 * cos + x1 * sin], axis=-1)
    return jnp.concatenate([rot.astype(x.dtype), x[..., ROPE_DIM:]], axis=-1)

def hgrn2_mixer(h, w_in, lower_bound, g_norm, w_out):
    B, T, _ = h.shape
    nC = T // CHUNK
    proj = h @ w_in
    q, f, i, g = jnp.split(proj, [HG_KEY_TOT, 2 * HG_KEY_TOT, 2 * HG_KEY_TOT + D_MODEL], axis=-1)
    q = jax.nn.silu(q.astype(jnp.float32))
    lb = lower_bound.astype(jnp.float32)
    ff = f.astype(jnp.float32)
    log_f = jnp.log(lb + (1 - lb) * jax.nn.sigmoid(ff))
    k = (1 - lb) * jax.nn.sigmoid(-ff)

    def to_chunks(a, d):
        return a.reshape(B, nC, CHUNK, HG_HEADS, d).transpose(1, 0, 3, 2, 4)

    qc = to_chunks(q, HG_KEY)
    kc = to_chunks(k, HG_KEY)
    vc = to_chunks(i.astype(jnp.float32), HG_VAL)
    bc = jnp.cumsum(to_chunks(log_f, HG_KEY), axis=-2)
    causal = jnp.tril(jnp.ones((CHUNK, CHUNK), dtype=bool))[:, :, None]

    def step(S, xs):
        q_, k_, v_, b_ = xs
        diff = b_[:, :, :, None, :] - b_[:, :, None, :, :]
        decay = jnp.exp(jnp.where(causal, diff, -jnp.inf))
        A = jnp.einsum('bhtd,bhsd,bhtsd->bhts', q_, k_, decay)
        o = (jnp.einsum('bhts,bhsv->bhtv', A, v_)
             + jnp.einsum('bhtd,bhdv->bhtv', q_ * jnp.exp(b_), S))
        b_last = b_[:, :, -1:, :]
        S_new = (jnp.exp(b_last)[:, :, 0, :, None] * S
                 + jnp.einsum('bhsd,bhsv->bhdv', k_ * jnp.exp(b_last - b_), v_))
        return S_new, o

    S0 = jnp.zeros((B, HG_HEADS, HG_KEY, HG_VAL), jnp.float32)
    _, oc = lax.scan(step, S0, (qc, kc, vc, bc))
    o = oc.transpose(1, 0, 3, 2, 4).reshape(B, T, HG_HEADS, HG_VAL)
    o = o * lax.rsqrt(jnp.mean(o * o, axis=-1, keepdims=True) + NORM_EPS)
    o = o * g_norm.astype(jnp.float32).reshape(HG_HEADS, HG_VAL)
    o = o.reshape(B, T, D_MODEL) * jax.nn.sigmoid(g.astype(jnp.float32))
    return o.astype(h.dtype) @ w_out

def swa_sink_mixer(h, positions, w_qkv, b_qkv, sinks, w_out, b_out):
    B, T, _ = h.shape
    nC = T // CHUNK
    qkv = h @ w_qkv + b_qkv
    q, k, v = jnp.split(qkv, [SW_Q_HEADS * SW_HEAD_DIM,
                              (SW_Q_HEADS + SW_KV_HEADS) * SW_HEAD_DIM], axis=-1)
    q = partial_rotary(q.reshape(B, T, SW_Q_HEADS, SW_HEAD_DIM), positions)
    k = partial_rotary(k.reshape(B, T, SW_KV_HEADS, SW_HEAD_DIM), positions)
    v = v.reshape(B, T, SW_KV_HEADS, SW_HEAD_DIM)

    qb = q.reshape(B, nC, CHUNK, SW_KV_HEADS, SW_GROUP, SW_HEAD_DIM).astype(jnp.float32)

    def band(a):
        a = a.reshape(B, nC, CHUNK, SW_KV_HEADS, SW_HEAD_DIM).astype(jnp.float32)
        a = jnp.pad(a, ((0, 0), (WINDOW_CHUNKS - 1, 0), (0, 0), (0, 0), (0, 0)))
        return jnp.concatenate([a[:, j:j + nC] for j in range(WINDOW_CHUNKS)], axis=2)

    kband, vband = band(k), band(v)
    key_chunk = (jnp.arange(nC)[:, None] - (WINDOW_CHUNKS - 1)
                 + jnp.arange(WINDOW_CHUNKS * CHUNK)[None, :] // CHUNK)
    valid = (key_chunk >= 0)[None, :, None, None, None, :]

    s = jnp.einsum('bnqkgd,bnskd->bnkgqs', qb, kband) * (SW_HEAD_DIM ** -0.5)
    s = jnp.where(valid, s, -jnp.inf)
    sink = sinks.astype(jnp.float32).reshape(1, 1, SW_KV_HEADS, SW_GROUP, 1, 1)
    m = jnp.maximum(jnp.max(s, axis=-1, keepdims=True), sink)
    p = jnp.exp(s - m)
    probs = p / (jnp.sum(p, axis=-1, keepdims=True) + jnp.exp(sink - m))
    o = jnp.einsum('bnkgqs,bnskd->bnqkgd', probs, vband)
    o = o.reshape(B, T, SW_Q_HEADS * SW_HEAD_DIM).astype(h.dtype)
    return o @ w_out + b_out

def setup_inputs(seed: int = 0) -> dict:
    key = jax.random.key(seed)
    ks = jax.random.split(key, 24)
    D = D_MODEL

    def w(k, shape, fan_in):
        return jax.random.normal(k, shape, jnp.float32) * fan_in ** -0.5

    def small(k, shape, s=0.02):
        return jax.random.normal(k, shape, jnp.float32) * s

    offsets = jax.random.randint(ks[2], (BATCH, 1), 0, 64) * CHUNK
    positions = (offsets + jnp.arange(SEQ, dtype=jnp.int32)[None, :]).astype(jnp.int32)
    return {
        "x": jax.random.normal(ks[0], (BATCH, SEQ, D), jnp.float32),
        "c": jax.random.normal(ks[1], (BATCH, D), jnp.float32),
        "positions": positions,
        "ada_w": w(ks[3], (DEPTH, D, N_ADA * D), D),
        "ada_b": small(ks[4], (DEPTH, N_ADA * D)),
        "norm_g": 1.0 + small(ks[5], (DEPTH, 3, D)),
        "ffn1_w_gu": w(ks[6], (DEPTH, D, 2 * D_FF), D),
        "ffn1_w_down": w(ks[7], (DEPTH, D_FF, D), D_FF),
        "ffn2_w_gu": w(ks[8], (DEPTH, D, 2 * D_FF), D),
        "ffn2_w_down": w(ks[9], (DEPTH, D_FF, D), D_FF),
        "hg_w_in": w(ks[10], (N_HGRN, D, 2 * HG_KEY_TOT + 2 * D), D),
        "hg_lower_bounds": small(ks[11], (DEPTH + 1, HG_KEY_TOT), 0.1),
        "hg_norm_g": 1.0 + small(ks[12], (N_HGRN, D)),
        "hg_w_out": w(ks[13], (N_HGRN, D, D), D),
        "sw_w_qkv": w(ks[14], (N_SWA, D, (SW_Q_HEADS + 2 * SW_KV_HEADS) * SW_HEAD_DIM), D),
        "sw_b_qkv": small(ks[15], (N_SWA, (SW_Q_HEADS + 2 * SW_KV_HEADS) * SW_HEAD_DIM)),
        "sw_sinks": jax.random.normal(ks[16], (N_SWA, SW_Q_HEADS), jnp.float32),
        "sw_w_out": w(ks[17], (N_SWA, SW_Q_HEADS * SW_HEAD_DIM, D), SW_Q_HEADS * SW_HEAD_DIM),
        "sw_b_out": small(ks[18], (N_SWA, D)),
        "final_norm_g": 1.0 + small(ks[19], (D,)),
    }

def reference(x, c, positions, ada_w, ada_b, norm_g, ffn1_w_gu, ffn1_w_down,
              ffn2_w_gu, ffn2_w_down, hg_w_in, hg_lower_bounds, hg_norm_g, hg_w_out,
              sw_w_qkv, sw_b_qkv, sw_sinks, sw_w_out, sw_b_out, final_norm_g):
    lb_table = jnp.cumsum(jax.nn.softmax(hg_lower_bounds.astype(jnp.float32), axis=0), axis=0)
    c_act = jax.nn.silu(c)
    for i in range(DEPTH):
        ada = c_act @ ada_w[i] + ada_b[i]
        sh1, sc1, g1, sh2, sc2, g2, sh3, sc3, g3 = jnp.split(ada, N_ADA, axis=-1)
        h = modulate(rms_norm(x, norm_g[i, 0]), sh1, sc1)
        x = x + FFN_RES_WEIGHT * g1[:, None, :] * swiglu_ffn(h, ffn1_w_gu[i], ffn1_w_down[i])
        h = modulate(rms_norm(x, norm_g[i, 1]), sh2, sc2)
        j = i // N_MIXERS
        if i % N_MIXERS == 0:
            y = hgrn2_mixer(h, hg_w_in[j], lb_table[i], hg_norm_g[j], hg_w_out[j])
        else:
            y = swa_sink_mixer(h, positions, sw_w_qkv[j], sw_b_qkv[j], sw_sinks[j],
                               sw_w_out[j], sw_b_out[j])
        x = x + g2[:, None, :] * y
        h = modulate(rms_norm(x, norm_g[i, 2]), sh3, sc3)
        x = x + FFN_RES_WEIGHT * g3[:, None, :] * swiglu_ffn(h, ffn2_w_gu[i], ffn2_w_down[i])
    return rms_norm(x, final_norm_g)


_drawn_inputs = setup_inputs


def setup_inputs(seed=0):
    import zlib

    import numpy as np

    out = dict(_drawn_inputs(seed))
    spreads = {}
    factors = {'norm_g': 3.182,
     'hg_lower_bounds': 8.0,
     'hg_norm_g': 8.0,
     'sw_b_qkv': 5.114,
     'sw_sinks': 64.0,
     'sw_b_out': 28.519,
     'final_norm_g': 8.316}
    for name, (base, spread) in spreads.items():
        noise = np.random.default_rng([zlib.crc32(name.encode()), seed]).standard_normal(out[name].shape)
        drawn = base * np.exp(spread * noise) if base else spread * noise
        out[name] = __import__('jax').numpy.asarray(drawn.astype(out[name].dtype))
    for name, factor in factors.items():
        out[name] = (out[name] * factor).astype(out[name].dtype)
    return out
```

```python
from contextlib import ExitStack

import numpy as np
import concourse.bass as bass
from concourse import mybir

ALU = mybir.AluOpType
ACT = mybir.ActivationFunctionType
AX = mybir.AxisListType.X
F32 = mybir.dt.float32
F32R = mybir.dt.float32r
I32 = mybir.dt.int32
U8 = mybir.dt.uint8

P = 128
D = 1024
T = 256
KT = D // P
TG = T // P
DFF = 2816
NF = DFF // P
NIT = NF // 2
UNIT = 2048
HALF = UNIT // 2
RAW = 6
JOBS = 6
EPS = 1e-6
CH = 64
NP_HG = 4
LEVELS = 8
ADA_UNITS = 72
HALF_ROPE = 8
MAGIC = 12582912.0

FFN_UNITS = 3 * NIT
UNIT_BASE = {"ffn0": 0}
UNIT_BASE["hgrn"] = UNIT_BASE["ffn0"] + FFN_UNITS
UNIT_BASE["ffn1"] = UNIT_BASE["hgrn"] + 20
UNIT_BASE["ffn2"] = UNIT_BASE["ffn1"] + FFN_UNITS
UNIT_BASE["swa"] = UNIT_BASE["ffn2"] + FFN_UNITS
UNIT_BASE["ffn3"] = UNIT_BASE["swa"] + 10
ADA_START = 8
ADA_FFN = {0: (8, 2), 1: (36, 2), 2: (58, 1), 3: (72, 0)}
ADA_HGRN = 30
HG_ADA = [0, 1, 2, 12, 13, 15]
ADA_SWA = 69

C_NORM, C_FINAL, C_LB, C_HGN, C_BQ, C_BO, C_C, C_ROWS = 0, 48, 56, 80, 88, 98, 106, 114
K_ID, K_PERM, K_DUP, K_FREQ, K_COLS = 0, 128, 256, 768, 769


def constants():
    k = np.zeros((P, K_COLS), np.float32)
    masks = np.zeros((P, 7 * 64), np.float32)
    for t in range(2):
        for p in range(P):
            k[64 * t + p % 64, K_DUP + t * P + p] = 1.0
    k[:, K_ID:K_ID + P] = np.eye(P, dtype=np.float32)
    for p in range(P):
        r = p % 64
        if r < HALF_ROPE:
            k[p + HALF_ROPE, K_PERM + p] = -1.0
        elif r < 2 * HALF_ROPE:
            k[p - HALF_ROPE, K_PERM + p] = 1.0
        if r < 2 * HALF_ROPE:
            for t in range(2):
                sign, at = (-1.0, r + HALF_ROPE) if r < HALF_ROPE else (1.0, r - HALF_ROPE)
                k[64 * t + at, K_DUP + (2 + t) * P + p] = sign
            k[p, K_FREQ] = np.float32(500000.0) ** (-np.float32(r % HALF_ROPE) / np.float32(HALF_ROPE))
    for lev in range(7):
        h = 1 << lev
        for s in range(P):
            if (s // h) % 2 == 0:
                n = s // (2 * h)
                masks[s, 64 * lev + n * h:64 * lev + (n + 1) * h] = 1.0
    return k, masks


def ffn_job(it, what, last=NIT - 1):
    if what == "G0":
        return 6 * it - 1 if it else 0
    if what == "U0":
        return 6 * it if it else 1
    if what == "D1":
        return 6 * it + (5 if it == last else 7)
    return 6 * it + {"G1": 2, "U1": 3, "D0": 4}[what]


def hgrn_steps():
    out = []
    for w in range(18):
        if w >= 6 and (w - 6) % 3 == 0:
            out.append((w, (w - 6) // 3, "O"))
        if w >= 7 and (w - 7) % 3 == 0 and (w - 7) // 3 < NP_HG:
            out.append((w, (w - 7) // 3, "S"))
        if 3 <= w < 15:
            p, g = (w - 3) // 3, (w - 3) % 3
            out += [(w, p, s) for s in (["D", 0, 1], [2, 3, 4], [5, 6, 7])[g]]
    return out


def trunk(nc, x, c, positions, ada_w, ada_b, norm_g, ffn1_w_gu, ffn1_w_down, ffn2_w_gu, ffn2_w_down,
          hg_w_in, hg_lower_bounds, hg_norm_g, hg_w_out, sw_w_qkv, sw_b_qkv, sw_sinks, sw_w_out,
          sw_b_out, final_norm_g, consts, masks, out):
    STEPS = hgrn_steps()
    STEP_AT = {(p, s): i for i, (_, p, s) in enumerate(STEPS)}

    with ExitStack() as ctx:
        def sb(name, shape, dt=F32):
            return ctx.enter_context(nc.sbuf_tensor(name, shape, dt))

        def sem(name):
            return ctx.enter_context(nc.semaphore(name))

        raw = sb("raw", [P, RAW, UNIT])
        ada_raw = sb("ada_raw", [P, 2, UNIT])
        w_hi = sb("w_hi", [P, JOBS, HALF], F32R)
        w_lo = sb("w_lo", [P, JOBS, HALF], F32R)
        xT = sb("xT", [P, KT, T])
        h_hi = sb("h_hi", [P, KT, T], F32R)
        h_lo = sb("h_lo", [P, KT, T], F32R)
        mix = sb("mix", [P, KT, T])
        sq = sb("sq", [P, 4, T])
        xr = sb("xr", [P, 4, T])
        hf = sb("hf", [P, 4, T])
        sd = sb("sd", [P, T])
        rstd = sb("rstd", [P, T])
        sil = sb("sil", [P, 2, T])
        act_f = sb("act_f", [P, 2, T])
        a_hi = sb("a_hi", [P, 2, T], F32R)
        a_lo = sb("a_lo", [P, 2, T], F32R)
        acc = sb("acc", [P, T])
        con = sb("con", [P, K_COLS])
        mask_t = sb("mask_t", [P, 7, 64], U8)
        ones = sb("ones", [P, P])
        inv_d = sb("inv_d", [P, P])
        eps_t = sb("eps_t", [P, 1])
        stage = sb("stage", [P, 3, P])
        adab = sb("adab", [P, 144])
        adac = sb("adac", [P, 144])
        vec = sb("vec", [P, C_ROWS])
        c_act = sb("c_act", [P, KT])
        scol = sb("scol", [P, KT])
        gcol = sb("gcol", [P, KT])
        small = sb("small", [P, 8, KT])
        lb = sb("lb", [P, KT])
        oml = sb("oml", [P, KT])
        sink = sb("sink", [P, KT])
        sink_all = sb("sink_all", [P, 2 * KT])
        bv = sb("bv", [P, T])
        cosb = sb("cosb", [P, T])
        sinb = sb("sinb", [P, T])
        shared = [v for tile_ in (sq, xr, hf) for v in (tile_[:, 0:2, :], tile_[:, 2:4, :])]
        m512 = shared + [sb(f"m512_{i}", [P, 2, T]) for i in range(12)]
        stat = sb("stat", [P, 2, 8, 4])

        psum = [ctx.enter_context(nc.psum_tensor(f"bank{i}", [P, 512], F32)) for i in range(8)]
        SUMS, ADA_BANK = 7, 6

        def y_acc(m):
            return psum[m // 2][:, (m % 2) * T:(m % 2 + 1) * T]

        def y_pair(m):
            return psum[4 + (m // 2) % 2][:, (m % 2) * T:(m % 2 + 1) * T]

        raw_landed = [sem(f"raw_landed{i}") for i in range(RAW)]
        ada_landed = [sem(f"ada_landed{i}") for i in range(2)]
        w_hi_ready = sem("w_hi_ready")
        w_lo_ready = sem("w_lo_ready")
        w_used = sem("w_used")
        ada_step = sem("ada_step")
        ada_sum = sem("ada_sum")
        ada_out = sem("ada_out")
        small_in = sem("small_in")
        x_in = sem("x_in")
        const_in = sem("const_in")
        const_set = sem("const_set")
        stage_t = sem("stage_t")
        vec_ready = sem("vec_ready")
        c_ready = sem("c_ready")
        dve_link = sem("dve_link")
        act_link = sem("act_link")
        angle = sem("angle")
        y_done = sem("y_done")
        x_ready = sem("x_ready")
        sq_ready = sem("sq_ready")
        ss_done = sem("ss_done")
        sd_ready = sem("sd_ready")
        xr_ready = sem("xr_ready")
        cols_ready = sem("cols_ready")
        hf_ready = sem("hf_ready")
        h_hi_ready = sem("h_hi_ready")
        h_lo_ready = sem("h_lo_ready")
        silu_done = sem("silu_done")
        a_mul = sem("a_mul")
        a_hi_ready = sem("a_hi_ready")
        a_lo_ready = sem("a_lo_ready")
        proj_read = sem("proj_read")
        gates_used = sem("gates_used")
        chain_in = sem("chain_in")
        chain_mm = sem("chain_mm")
        chain_read_dve = sem("chain_read_dve")
        osq_ready = sem("osq_ready")
        osd_ready = sem("osd_ready")
        o_normed = sem("o_normed")
        mix_hi = sem("mix_hi")
        mix_lo = sem("mix_lo")
        sw_evac = sem("sw_evac")
        sw_v = sem("sw_v")
        rope_mm = sem("rope_mm")
        rope_done = sem("rope_done")
        s_mm = sem("s_mm")
        s_max = sem("s_max")
        p_exp = sem("p_exp")
        p_norm = sem("p_norm")
        pt_mm = sem("pt_mm")
        pt_copied = sem("pt_copied")
        o_mm = sem("o_mm")
        out_t = sem("out_t")
        out_copied = sem("out_copied")
        stored = sem("stored")

        def cols(w, c0, n=256):
            return w.rearrange("(k p) c -> p k c", p=P)[:, :, bass.ds(c0, n)]

        GU = [ffn1_w_gu[0], ffn2_w_gu[0], ffn1_w_gu[1], ffn2_w_gu[1]]
        DOWN = [ffn1_w_down[0], ffn2_w_down[0], ffn1_w_down[1], ffn2_w_down[1]]
        HG_COL = [(w // 3) * 256 + (w % 3) * D if w < 12 else 3 * D + (w - 12) * 256 for w in range(16)]
        SW_COL = [D, D + 256, 0, 256, 512, 768]
        POST = {0: "ffn0", 1: "hgrn", 2: "ffn1", 3: "ffn2", 4: "swa", 5: "ffn3"}

        def gu_count(n, it, hf_):
            return 2 * UNIT_BASE[f"ffn{n}"] + ffn_job(it, f"G{hf_}") + 2

        def down_count(n, it, hf_):
            return 2 * UNIT_BASE[f"ffn{n}"] + ffn_job(it, f"D{hf_}") + 1

        def split_count(unit):
            for n in range(4):
                u = UNIT_BASE[f"ffn{n}"]
                if u <= unit < u + FFN_UNITS:
                    it, r = divmod(unit - u, 3)
                    return 2 * u + ffn_job(it, ("G1", "U1", "D1")[r]) + 1
            return 2 * unit + 2

        Y_STAGES = [0, 1, 3, 4, 6]

        def y_wait(eng, b, m):
            m |= 1
            if b in (2, 5):
                eng.wait_ge(w_used, 2 * (UNIT_BASE["hgrn"] + 16 if b == 2 else UNIT_BASE["swa"] + 6) + m + 1)
            else:
                eng.wait_ge(y_done, 8 * Y_STAGES.index(b) + m + 1)

        def raw_cols(slot):
            return raw[:, slot, :].rearrange("p (k c) -> p k c", k=KT)

        def even(u, i):
            return u % RAW, u // RAW + i

        block = ctx.enter_context(nc.Block())

        @block.sync
        def _(sp):
            def load_unit(u, src, i=0, k=KT, free_at=None):
                slot, turn = even(u, i)
                if u >= RAW:
                    sp.wait_ge(w_lo_ready, free_at + 12 * i if free_at is not None else split_count(u - RAW))
                sp.dma_start(raw[:, slot, :].rearrange("p (k c) -> p k c", k=k), src).then_inc(raw_landed[slot], 16)

            def load_ada(a, i=0):
                slot = a % 2
                if a >= 2:
                    sp.wait_ge(ada_step, 8 * (a - 1) + 16 * i)
                layer = a // 36
                src = cols(ada_w[layer], (a % 36) * 256 + i * 512)
                sp.dma_start(ada_raw[:, slot, :].rearrange("p (k c) -> p k c", k=KT), src)\
                    .then_inc(ada_landed[slot], 16)

            sp.dma_start(con[:, :], consts).then_inc(const_in, 16)
            sp.dma_start(hf[:, 0:2, :].rearrange("p a t -> p (a t)")[:, 0:448], masks).then_inc(const_in, 16)
            for layer in range(2):
                sp.dma_start(stage[0:72, layer, :], ada_b[layer].rearrange("(a b) -> a b", b=P)).then_inc(small_in, 16)
            rows = [(C_NORM, norm_g.rearrange("l s (a b) -> (l s a) b", b=P)),
                    (C_FINAL, final_norm_g.rearrange("(a b) -> a b", b=P)),
                    (C_LB, hg_lower_bounds.rearrange("l (a b) -> (l a) b", b=P)),
                    (C_HGN, hg_norm_g[0].rearrange("(a b) -> a b", b=P)),
                    (C_BQ, sw_b_qkv[0, 0:D + 256].rearrange("(a b) -> a b", b=P)),
                    (C_BO, sw_b_out[0].rearrange("(a b) -> a b", b=P)),
                    (C_C, c[0].rearrange("(a b) -> a b", b=P))]
            for r, src in rows:
                sp.dma_start(stage[r:r + src.shape[0], 2, :], src).then_inc(small_in, 16)
            load_ada(0)
            load_ada(1)
            sp.dma_start(mix[:, :, :].rearrange("p (g a) t -> p g (a t)", g=TG),
                         x[0].rearrange("(g p) d -> p g d", p=P)).then_inc(x_in, 16)
            pos = positions[0:1, :].broadcast_to([P, T])
            sp.dma_start(sinb[:, :].bitcast(I32), pos).then_inc(x_in, 16)
            sp.dma_start(bv[:, :], sw_b_qkv[0:1, D + 256:D + 512].broadcast_to([P, T])).then_inc(x_in, 16)
            sp.dma_start(sink_all[:, :], sw_sinks.broadcast_to([P, 2 * KT])).then_inc(x_in, 16)
            for a in range(2, ADA_START):
                load_ada(a)

            def ffn_loads(n, it, i=0):
                u = UNIT_BASE[f"ffn{n}"] + 3 * it
                free = [2 * UNIT_BASE[f"ffn{n}"] + 6 * (it - 2) + j + 1 for j in (2, 3, 7)] if it else [None] * 3
                c0 = it * 256 + i * 512
                ada0, per = ADA_FFN[n]
                load_unit(u, cols(GU[n], c0), i, free_at=free[0])
                load_unit(u + 1, cols(GU[n], c0 + DFF), i, free_at=free[1])
                if per == 2:
                    a = ada0 + 2 * it
                    for t in range(2):
                        ada_in_loop(a + t, i, 4)
                elif per == 1:
                    ada_in_loop(ada0 + it, i, 2)
                load_unit(u + 2, DOWN[n].rearrange("(a p) c -> p a c", p=P)[:, bass.ds(2 * it + 4 * i, 2), :], i, 2,
                          free_at=free[2])

            def ada_in_loop(a, i, per):
                slot = a % 2
                if a >= 2:
                    sp.wait_ge(ada_step, 8 * (a - 1) + 8 * per * i)
                layer = a // 36
                src = cols(ada_w[layer], (a % 36) * 256 + i * 256 * per)
                sp.dma_start(ada_raw[:, slot, :].rearrange("p (k c) -> p k c", k=KT), src)\
                    .then_inc(ada_landed[slot], 16)

            def ffn_stream(n):
                ffn_loads(n, 0)
                with sp.Fori(0, (NIT - 3) // 2) as i:
                    ffn_loads(n, 1, i)
                    ffn_loads(n, 2, i)
                ffn_loads(n, NIT - 2)
                ffn_loads(n, NIT - 1)

            ffn_stream(0)
            for w in range(16):
                load_unit(UNIT_BASE["hgrn"] + w, cols(hg_w_in[0], HG_COL[w]))
                if w in HG_ADA:
                    load_ada(ADA_HGRN + HG_ADA.index(w))
            for w in range(4):
                load_unit(UNIT_BASE["hgrn"] + 16 + w, cols(hg_w_out[0], w * 256))
            ffn_stream(1)
            ffn_stream(2)
            for w in range(6):
                load_unit(UNIT_BASE["swa"] + w, cols(sw_w_qkv[0], SW_COL[w]))
                if w < 3:
                    load_ada(ADA_SWA + w)
            for w in range(4):
                load_unit(UNIT_BASE["swa"] + 6 + w, cols(sw_w_out[0], w * 256))
            ffn_stream(3)
            sp.wait_ge(out_copied, 2 * KT)
            sp.dma_start(out[0].rearrange("(g p) d -> p g d", p=P),
                         mix[:, :, :].rearrange("p (g a) t -> p g (a t)", g=TG)).then_inc(stored, 16)
            sp.wait_ge(stored, 16)

        q_t, k_t, f_t = m512[0:2], m512[2:4], m512[4:6]
        r_t, kl_t = m512[6], m512[7:9]
        v_t = m512[9:11]
        at_t = m512[11:13]
        sg_t = m512[13:15]
        o_t, osd_t = m512[15], m512[16]
        ql_t = m512[17]

        rq_t, rk_t = m512[0:4], m512[4:6]
        vt_t, vmix_t = m512[6], m512[7]
        raw_t = m512[8:10]
        rope_t = m512[10:12]
        p_t, pt_t = m512[12:14], m512[14:16]
        at2_t = sb("at2_t", [P, 2, 2, P])

        def raw_half(slot, half, kind):
            if kind == "D":
                return raw[:, slot, half * HALF:(half + 1) * HALF]
            return raw_cols(slot)[:, :, half * P:(half + 1) * P]

        def ring_half(ring, slot, kind):
            v = ring[:, slot, :]
            return v if kind == "D" else v.rearrange("p (k c) -> p k c", k=KT)

        def split_hi(act, job, unit, half, kind, i=0):
            slot, turn = even(unit, i)
            act.wait_ge(raw_landed[slot], 16 * (turn + 1))
            if job >= JOBS:
                act.wait_ge(w_used, job + 12 * i - JOBS + 1)
            nc.scalar.activation(ring_half(w_hi, job % JOBS, kind), raw_half(slot, half, kind), ACT.Copy)\
                .then_inc(w_hi_ready, 1)

        def split_lo(dve, job, unit, half, kind, i=0):
            slot = unit % RAW
            dve.wait_ge(w_hi_ready, job + 12 * i + 1)
            ins = nc.vector.tensor_tensor(ring_half(w_lo, job % JOBS, kind), raw_half(slot, half, kind),
                                          ring_half(w_hi, job % JOBS, kind).bitcast(F32), ALU.subtract)
            ins.then_inc(w_lo_ready, 1)

        def first_jobs(stage_no):
            name = POST[stage_no]
            u = UNIT_BASE[name]
            if name.startswith("ffn"):
                return [(2 * u, u, 0, "C"), (2 * u + 1, u + 1, 0, "C")]
            return [(2 * u, u, 0, "C"), (2 * u + 1, u, 1, "C")]

        def unit_jobs(u):
            return [(2 * u, u, 0, "C"), (2 * u + 1, u, 1, "C")]

        def half_jobs(n, it, hf_):
            u = UNIT_BASE[f"ffn{n}"]
            jb = 2 * u
            if hf_ == 0:
                return [(jb + ffn_job(it, "G1"), u + 3 * it, 1, "C"), (jb + ffn_job(it, "U1"), u + 3 * it + 1, 1, "C"),
                        (jb + ffn_job(it, "D0"), u + 3 * it + 2, 0, "D")]
            jobs = []
            if it < NIT - 1:
                jobs = [(jb + ffn_job(it + 1, "G0"), u + 3 * it + 3, 0, "C"),
                        (jb + ffn_job(it + 1, "U0"), u + 3 * it + 4, 0, "C")]
            return jobs + [(jb + ffn_job(it, "D1"), u + 3 * it + 2, 1, "D")]

        def ada_of(n, it, hf_):
            ada0, per = ADA_FFN[n]
            if per == 2:
                return ada0 + 2 * it + hf_, 4
            if per == 1 and hf_ == 0:
                return ada0 + it, 2
            return None, 0

        def chain_bank(c_):
            return psum[(4, 5, 7)[c_ % 3]][:, :].rearrange("p (a t) -> p a t", a=2)

        RING45 = [("C", 0), ("R", 0), ("C", 1)] + [("R", i) for i in range(1, 5)] + [("S", 0), ("R", 5)] + [("S", i) for i in range(1, 8)]
        RING_AT = {k: i for i, k in enumerate(RING45)}

        def s_bank(b):
            return 4 + RING_AT[("S", b)] % 2

        def r_bank(r):
            return 4 + RING_AT[("R", r)] % 2

        def p_block(b):
            return p_t[b % 2][:, :, :].rearrange("p a (b t) -> p (a b) t", b=2)

        def pt_block(b):
            return pt_t[b % 2][:, :, :].rearrange("p a (b t) -> p (a b) t", b=2)

        def h_count(b):
            return 8 * b

        def at_view(p):
            return at_t[p % 2][:, :, :].rearrange("p a (g t) -> p a g t", g=TG)

        def ql_view(s):
            return ql_t[:, s % 2, :].rearrange("p (a t) -> p a t", a=2)

        @block.scalar
        def _(act):
            link = [0]

            def linked(ins):
                link[0] += 1
                ins.then_inc(act_link, 1)
                act.wait_ge(act_link, link[0])

            act.wait_ge(vec_ready, 3)
            nc.scalar.activation(c_act[:, :], vec[:, C_C:C_C + KT], ACT.Silu).then_inc(c_ready, 1)
            act.wait_ge(const_set, 6)
            nc.scalar.activation(small[:, 0:3, :], small[:, 0:3, :], ACT.Exp).then_inc(c_ready, 1)
            act.wait_ge(angle, 1)
            nc.scalar.activation(cosb[:, :], xr[:, 0, :], ACT.Sin).then_inc(c_ready, 1)
            nc.scalar.activation(sinb[:, :], xr[:, 1, :], ACT.Sin).then_inc(c_ready, 1)

            def stage_part(b):
                if b < 6:
                    for j in first_jobs(b):
                        split_hi(act, *j)
                for m in range(KT):
                    act.wait_ge(x_ready, 8 * b + m + 1)
                    if b or m >= 4:
                        act.wait_ge(ss_done, 8 * b + m - 3)
                    nc.scalar.activation(sq[:, m % 4, :], xT[:, m, :], ACT.Square).then_inc(sq_ready, 1)
                act.wait_ge(ss_done, 8 * b + 8)
                nc.scalar.activation(sd[:, :], psum[SUMS][:, 0:T], ACT.Sqrt, bias=eps_t[:, 0:1])\
                    .then_inc(sd_ready, 1)
                act.wait_ge(cols_ready, b + 1)
                for m in range(KT):
                    act.wait_ge(xr_ready, 8 * b + m + 1)
                    g = 8 * b + m
                    if b < 6:
                        if g >= 4:
                            act.wait_ge(h_lo_ready, g - 3)
                    elif m >= 4:
                        act.wait_ge(out_t, 2 * (m - 3))
                    else:
                        act.wait_ge(h_lo_ready, g - 3)
                    if b < 6:
                        s = b % 3
                        sh = (b // 3) * 72 + 24 * s + m
                        nc.scalar.activation(hf[:, m % 4, :], xr[:, m % 4, :], ACT.Identity,
                                             scale=scol[:, m:m + 1], bias=adac[:, sh:sh + 1]).then_inc(hf_ready, 1)
                        act.wait_ge(hf_ready, g + 1)
                        nc.scalar.activation(h_hi[:, m, :], hf[:, m % 4, :], ACT.Copy).then_inc(h_hi_ready, 1)
                    else:
                        nc.scalar.activation(hf[:, m % 4, :], xr[:, m % 4, :], ACT.Copy,
                                             scale=scol[:, m:m + 1]).then_inc(hf_ready, 1)
                        if m:
                            out_evac(m - 1)
                if b == 6:
                    out_evac(KT - 1)

            def out_evac(m):
                act.wait_ge(out_t, 2 * m + 2)
                dst = mix[:, :, :].rearrange("p (g a) t -> p g (a t)", g=TG)[:, :, m * P:(m + 1) * P]
                nc.scalar.activation(dst, psum[m % 4][:, 0:T].rearrange("p (g t) -> p g t", g=TG), ACT.Copy)\
                    .then_inc(out_copied, 2)

            def ffn_half(n, it, hf_, i=0):
                for j in half_jobs(n, it, hf_):
                    split_hi(act, *j, i=i)
                g = NF * n + 2 * it + hf_
                act.wait_ge(w_used, gu_count(n, it, hf_) + 12 * i)
                nc.scalar.activation(sil[:, hf_, :], psum[4 + hf_][:, 0:T], ACT.Silu).then_inc(silu_done, 1)
                act.wait_ge(a_mul, g + 4 * i + 1)
                if it:
                    act.wait_ge(w_used, down_count(n, it - 1, hf_) + 12 * i)
                nc.scalar.activation(a_hi[:, hf_, :], act_f[:, hf_, :], ACT.Copy).then_inc(a_hi_ready, 1)

            def ffn(n):
                for hf_ in range(2):
                    ffn_half(n, 0, hf_)
                with act.Fori(0, (NIT - 3) // 2) as i:
                    for it in (1, 2):
                        for hf_ in range(2):
                            ffn_half(n, it, hf_, i)
                for it in (NIT - 2, NIT - 1):
                    for hf_ in range(2):
                        ffn_half(n, it, hf_)

            def hgrn():
                u = UNIT_BASE["hgrn"]
                evac = [0]

                def proj_evac(w):
                    bank = psum[w % 4][:, :].rearrange("p (a t) -> p a t", a=2)
                    act.wait_ge(w_used, 2 * (u + w + 1))
                    if w < 12 and w % 3 == 2:
                        p = w // 3
                        if p >= 2:
                            act.wait_ge(chain_mm, STEP_AT[(p - 2, "O")] + 1)
                        nc.scalar.activation(v_t[p % 2][:, :, :], bank, ACT.Copy).then_inc(proj_read, 1)
                        return
                    if evac[0]:
                        act.wait_ge(gates_used, evac[0])
                    evac[0] += 1
                    ins = nc.scalar.activation(sg_t[0][:, :, :], bank, ACT.Sigmoid)
                    if w < 12 and w % 3 == 0:
                        ins = nc.scalar.activation(sg_t[1][:, :, :], bank, ACT.Copy)
                    elif w < 12:
                        ins = nc.scalar.activation(sg_t[1][:, :, :], bank, ACT.Sigmoid, scale=-1.0)
                    ins.then_inc(proj_read, 1)

                for w in range(18):
                    if w + 1 < 20 and w < 17:
                        for j in unit_jobs(u + w + 1):
                            split_hi(act, *j)
                    if 1 <= w <= 16:
                        proj_evac(w - 1)
                    for c_, (ws, p, s) in enumerate(STEPS):
                        if ws != w:
                            continue
                        if s == "O":
                            act.wait_ge(chain_mm, c_ + 1)
                            if p:
                                act.wait_ge(o_normed, p)
                            nc.scalar.activation(o_t[:, :, :], chain_bank(c_), ACT.Copy)
                            nc.scalar.activation(osd_t[:, :, :], chain_bank(c_), ACT.Square)\
                                .then_inc(osq_ready, 1)
                        if s == "S":
                            act.wait_ge(chain_mm, c_ + 1)
                            nc.scalar.activation(osd_t[:, :, :], chain_bank(c_), ACT.Sqrt, scale=8.0,
                                                 bias=eps_t[:, 0:1]).then_inc(osd_ready, 1)
                act.wait_ge(w_used, 2 * (u + 16))
                for p in range(NP_HG):
                    act.wait_ge(gates_used, 2 * NP_HG + p + 1)
                    nc.scalar.activation(h_hi[:, 2 * p:2 * p + 2, :], mix[:, 2 * p:2 * p + 2, :], ACT.Copy)\
                        .then_inc(mix_hi, 1)
                for w in range(18, 20):
                    for j in unit_jobs(u + w):
                        split_hi(act, *j)

            def swa():
                u = UNIT_BASE["swa"]

                def evac(w):
                    if w == 1:
                        return
                    act.wait_ge(w_used, 2 * (u + w + 1))
                    i = w - 1 if w else 0
                    bank = psum[0 if w == 0 else (2 + i) % 4]
                    col = C_BQ + (2 * (i - 1) if w else KT)
                    if i >= 2:
                        act.wait_ge(rope_done, i)
                    for t in range(2):
                        nc.scalar.activation(raw_t[i % 2][:, t, :], bank[:, t * T:(t + 1) * T], ACT.Identity,
                                             bias=vec[:, col + t:col + t + 1]).then_inc(sw_evac, 1)

                def softmax(b):
                    n = b % 4
                    keys = CH if n == 0 else 2 * CH
                    act.wait_ge(s_max, b + 1)
                    if b >= 2:
                        act.wait_ge(pt_mm, b - 1)
                    for j in range(4):
                        nc.scalar.activation(p_block(b)[:, j, 0:keys], psum[s_bank(b)][:, j * P:j * P + keys],
                                             ACT.Exp, scale=0.125, bias=stat[:, b % 2, 2, j:j + 1],
                                             accum_out=stat[:, b % 2, 4, j:j + 1]).then_inc(p_exp, 1)
                    nc.scalar.activation(stat[:, b % 2, 5, :], stat[:, b % 2, 3, :], ACT.Exp).then_inc(p_exp, 1)

                def pt_copy(b):
                    keys = CH if b % 4 == 0 else 2 * CH
                    act.wait_ge(pt_mm, b + 1)
                    if b >= 2:
                        act.wait_ge(o_mm, b - 1)
                    nc.scalar.activation(pt_t[b % 2][0:keys, :, :],
                                         psum[6 + b % 2][0:keys, :].rearrange("p (a t) -> p a t", a=2), ACT.Copy)\
                        .then_inc(pt_copied, 1)

                for w in range(7):
                    if w + 1 < 8:
                        for j in unit_jobs(u + w + 1):
                            split_hi(act, *j)
                    if w >= 1:
                        evac(w - 1)
                for b in range(10):
                    if b < 8:
                        softmax(b)
                    if 1 <= b < 9:
                        pt_copy(b - 1)
                    if b in (5, 9):
                        for jp in range(2):
                            o_split(4 * (b == 9) // 2 + jp, b)
                for w in range(8, 10):
                    for j in unit_jobs(u + w):
                        split_hi(act, *j)

            def o_split(jp, b):
                act.wait_ge(o_mm, 4 if b == 5 else 8)
                nc.scalar.activation(h_hi[:, 2 * jp:2 * jp + 2, :], psum[jp][:, :].rearrange("p (a t) -> p a t", a=2),
                                     ACT.Copy).then_inc(mix_hi, 1)

            stage_part(0)
            ffn(0)
            stage_part(1)
            hgrn()
            stage_part(2)
            ffn(1)
            stage_part(3)
            ffn(2)
            stage_part(4)
            swa()
            stage_part(5)
            ffn(3)
            stage_part(6)

        @block.tensor
        def _(pe):
            def product(dst, hi, lo, rhi, rlo, first, last, group=False):
                nc.tensor.matmul(dst, hi, rhi, start=first, stop=False, skip_group_check=group)
                nc.tensor.matmul(dst, hi, rlo, start=False, stop=False, skip_group_check=group)
                return nc.tensor.matmul(dst, lo, rhi, start=False, stop=last, skip_group_check=group)

            def w_tiles(job, k):
                s = job % JOBS
                return w_hi[:, s, k * P:(k + 1) * P], w_lo[:, s, k * P:(k + 1) * P]

            pe.wait_ge(const_in, 32)
            pe.wait_ge(small_in, 16 * 9)
            for t, n in ((0, 72), (1, 72), (2, C_ROWS)):
                nc.tensor.transpose(psum[4][:, t * P:t * P + n], stage[0:n, t, :], con[0:n, K_ID:K_ID + n])\
                    .then_inc(stage_t, 1)
            pe.wait_ge(x_in, 16 * 4)
            xin = mix[:, :, :].rearrange("p (g a) t -> p g (a t)", g=TG)
            for m in range(KT):
                for g in range(TG):
                    ins = nc.tensor.transpose(y_acc(m)[:, g * P:(g + 1) * P], xin[:, g, m * P:(m + 1) * P],
                                              con[:, K_ID:K_ID + P])
                ins.then_inc(y_done, 1)
            pe.wait_ge(const_set, 6)

            def ada_reduce(a, step=0, i=0):
                pe.wait_ge(ada_step, 8 * a + 8 * step * i + 8)
                if a:
                    pe.wait_ge(ada_out, a + step * i)
                col = 2 * (a % 2)
                for t in range(2):
                    ins = nc.tensor.matmul(psum[ADA_BANK][:, col + t:col + t + 1], acc[:, t * P:(t + 1) * P],
                                           ones[:, 0:1], start=True, stop=True)
                ins.then_inc(ada_sum, 1)

            for a in range(ADA_START):
                ada_reduce(a)

            def stage_part(b):
                for m in range(KT):
                    pe.wait_ge(sq_ready, 8 * b + m + 1)
                    if b and m == 0:
                        pe.wait_ge(sd_ready, b)
                    nc.tensor.matmul(psum[SUMS][:, 0:T], inv_d[:, :], sq[:, m % 4, :], start=(m == 0),
                                     stop=(m == KT - 1)).then_inc(ss_done, 1)

            def gate_up(n, it, hf_, i=0):
                u = UNIT_BASE[f"ffn{n}"]
                jg = 2 * u + ffn_job(it, f"G{hf_}")
                b = (0, 2, 3, 5)[n]
                g = NF * n + 2 * it + hf_
                pe.wait_ge(w_lo_ready, jg + 12 * i + 2)
                if g >= 2:
                    pe.wait_ge(a_mul, g + 4 * i - 1)
                for k in range(KT):
                    if it == 0 and hf_ == 0:
                        pe.wait_ge(h_lo_ready, h_count(b) + k + 1)
                    for t in range(2):
                        hi, lo = w_tiles(jg + t, k)
                        ins = product(psum[4 + hf_][:, t * T:(t + 1) * T], hi, lo, h_hi[:, k, :], h_lo[:, k, :],
                                      k == 0 and t == 0, k == KT - 1, group=True)
                ins.then_inc(w_used, 2)

            def down(n, it, hf_, i=0, first=False, last=False):
                u = UNIT_BASE[f"ffn{n}"]
                job = 2 * u + ffn_job(it, f"D{hf_}")
                g = NF * n + 2 * it + hf_
                pe.wait_ge(w_lo_ready, job + 12 * i + 1)
                pe.wait_ge(a_lo_ready, g + 4 * i + 1)
                for m in range(KT):
                    hi, lo = w_tiles(job, m)
                    ins = product(y_acc(m), hi, lo, a_hi[:, hf_, :], a_lo[:, hf_, :], first and m % 2 == 0, last,
                                  group=True)
                    if last:
                        ins.then_inc(y_done, 1)
                if last:
                    pe.wait_ge(y_done, 8 * Y_STAGES.index((1, 3, 4, 6)[n]) + 8)
                    pe.sem_inc(w_used, 1)
                else:
                    ins.then_inc(w_used, 1)

            def iteration(n, it, i=0):
                for hf_ in range(2):
                    gate_up(n, it, hf_, i)
                    if hf_ == 1:
                        down(n, it, 0, i, first=(it == 0))
                    elif it:
                        down(n, it - 1, 1, i)
                    a, step = ada_of(n, it, hf_)
                    if a is not None:
                        ada_reduce(a, step, i)

            def ffn(n):
                iteration(n, 0)
                with pe.Fori(0, (NIT - 3) // 2) as i:
                    for it in (1, 2):
                        iteration(n, it, i)
                iteration(n, NIT - 2)
                iteration(n, NIT - 1)
                down(n, NIT - 1, 1, last=True)

            def proj(unit, bank, b, first):
                for t in range(2):
                    pe.wait_ge(w_lo_ready, 2 * unit + t + 1)
                    for k in range(KT):
                        if first and t == 0:
                            pe.wait_ge(h_lo_ready, h_count(b) + k + 1)
                        hi, lo = w_tiles(2 * unit + t, k)
                        ins = product(bank[:, t * T:(t + 1) * T], hi, lo, h_hi[:, k, :], h_lo[:, k, :],
                                      k == 0, k == KT - 1)
                    if t == 0:
                        ins.then_inc(w_used, 1)
                ins.then_inc(w_used, 1)

            def proj_tokens(unit, bank):
                pe.wait_ge(w_lo_ready, 2 * unit + 2)
                s = (2 * unit) % JOBS
                for g in range(TG):
                    tok = slice(g * P, (g + 1) * P)
                    for k in range(KT):
                        wh = w_hi[:, s:s + 2, k * P:(k + 1) * P]
                        wl = w_lo[:, s:s + 2, k * P:(k + 1) * P]
                        ins = product(bank[:, g * T:(g + 1) * T], h_hi[:, k, tok], h_lo[:, k, tok], wh, wl,
                                      k == 0, k == KT - 1)
                ins.then_inc(w_used, 2)

            def out_proj(u, b):
                r = 4 * (b == 5)
                for mp in range(4):
                    unit = u + mp
                    for t in range(2):
                        m = 2 * mp + t
                        pe.wait_ge(w_lo_ready, 2 * unit + t + 1)
                        if mp >= 2 and t == 0:
                            pe.wait_ge(x_ready, 8 * b + 2 * (mp - 1))
                        for k in range(KT):
                            if m == 0:
                                pe.wait_ge(mix_lo, r + k // 2 + 1)
                            hi, lo = w_tiles(2 * unit + t, k)
                            ins = product(y_pair(m), hi, lo, h_hi[:, k, :], h_lo[:, k, :], k == 0, k == KT - 1)
                        ins.then_inc(w_used, 1)

            def hgrn():
                u = UNIT_BASE["hgrn"]

                def chain(c_, p, s):
                    if c_ >= 3:
                        _, pp, prev = STEPS[c_ - 3]
                        if prev == "O":
                            pe.wait_ge(osq_ready, pp + 1)
                        elif prev == "S":
                            pe.wait_ge(osd_ready, pp + 1)
                        else:
                            pe.wait_ge(chain_read_dve, sum(x_[2] not in ("O", "S") for x_ in STEPS[:c_ - 2]))
                    bank = chain_bank(c_)
                    q, k = q_t[p % 2], k_t[p % 2]
                    if s == "D":
                        pe.wait_ge(gates_used, 2 * p + 2)
                        for hh in range(2):
                            for g in range(TG):
                                tok = slice(g * P, (g + 1) * P)
                                ins = nc.tensor.matmul(bank[:, hh, tok], k[:, hh, tok], q[:, hh, tok],
                                                       start=True, stop=True)
                    elif s == "O":
                        pe.wait_ge(chain_read_dve, 9 * (p + 1))
                        pe.wait_ge(proj_read, 3 * p + 3)
                        v, at = v_t[p % 2], at_view(p)
                        for hh in range(2):
                            vc = slice(hh * P, (hh + 1) * P)
                            nc.tensor.matmul(bank[:, hh, 0:P], v[:, 0, vc], at[:, hh, 0, :], start=True, stop=True)
                            nc.tensor.matmul(bank[:, hh, P:T], v[:, 0, vc], at2_t[:, p % 2, hh, :],
                                             start=True, stop=False)
                            ins = nc.tensor.matmul(bank[:, hh, P:T], v[:, 1, vc], at[:, hh, 1, :],
                                                   start=False, stop=True)
                    elif s == "S":
                        pe.wait_ge(osq_ready, p + 1)
                        ins = nc.tensor.matmul(bank, inv_d[:, :], osd_t[:, :, :], start=True, stop=True)
                    else:
                        pe.wait_ge(chain_in, 8 * p + s + 1)
                        kl = k if s == 0 else kl_t[s % 2]
                        ql = ql_view(s)
                        for hh in range(2):
                            if s == 7:
                                ins = nc.tensor.matmul(bank[:, 0, hh * P:(hh + 1) * P], kl[:, hh, 0:P],
                                                       ql[:, hh, :], start=True, stop=True)
                                continue
                            for g in range(TG):
                                ins = nc.tensor.matmul(bank[:, 0, (hh * TG + g) * 64:(hh * TG + g + 1) * 64],
                                                       kl[:, hh, g * P:(g + 1) * P], ql[:, hh, g * 64:(g + 1) * 64],
                                                       start=True, stop=True)
                    ins.then_inc(chain_mm, 1)

                for w in range(18):
                    if w < 16:
                        if w >= 4:
                            pe.wait_ge(proj_read, w - 3)
                        if w < 12 and w % 3 == 2:
                            proj_tokens(u + w, psum[w % 4])
                        else:
                            proj(u + w, psum[w % 4], 1, w == 0)
                    for c_, (ws, p, s) in enumerate(STEPS):
                        if ws == w:
                            chain(c_, p, s)
                    if w in HG_ADA:
                        ada_reduce(ADA_HGRN + HG_ADA.index(w))
                out_proj(u + 16, 2)

            def swa():
                u = UNIT_BASE["swa"]

                def ring_wait(i):
                    if i < 2:
                        return
                    kind, j = RING45[i - 2]
                    if kind in "CR":
                        pe.wait_ge(rope_done, j + 1)
                    else:
                        pe.wait_ge(p_exp, 5 * (j + 1))

                def rotate(r):
                    pe.wait_ge(sw_evac, 2 * max(r, 1))
                    for what in ("C", "R") if r < 2 else ("R",):
                        ring_wait(RING_AT[(what, r)])
                        bank = psum[4 + RING_AT[(what, r)] % 2]
                        if r < 2:
                            for t in range(2):
                                c0 = K_DUP + (t if what == "C" else 2 + t) * P
                                ins = nc.tensor.matmul(bank[:, t * T:(t + 1) * T], con[:, c0:c0 + P],
                                                       raw_t[0][:, r, :], start=True, stop=True)
                        else:
                            ins = nc.tensor.matmul(bank[:, :].rearrange("p (a t) -> p a t", a=2),
                                                   con[:, K_PERM:K_PERM + P], raw_t[(r - 1) % 2][:, :, :],
                                                   start=True, stop=True)
                    ins.then_inc(rope_mm, 1)

                def scores(b):
                    jh, n = b // 4, b % 4
                    ring_wait(RING_AT[("S", b)])
                    pe.wait_ge(rope_done, 4 + 2 * jh)
                    key_runs = {0: [(0, 64)], 1: [(0, 128)], 2: [(128, 64), (64, 64)], 3: [(128, 128)]}[n]
                    for jj in range(4):
                        j = 4 * jh + jj
                        for hh in range(2):
                            half = slice(64 * hh, 64 * hh + 64)
                            col = jj * P
                            for k0, kn in key_runs:
                                ins = nc.tensor.matmul(psum[s_bank(b)][half, col:col + kn],
                                                       rq_t[j // 2][half, j % 2, n * CH:(n + 1) * CH],
                                                       rk_t[j // 4][half, (j // 2) % 2, k0:k0 + kn],
                                                       start=True, stop=True)
                                col += kn
                    ins.then_inc(s_mm, 1)

                def turn(b):
                    keys = CH if b % 4 == 0 else 2 * CH
                    pe.wait_ge(p_norm, b + 1)
                    if b >= 2:
                        pe.wait_ge(pt_copied, b - 1)
                    elif b == 0:
                        pe.wait_ge(ada_out, ADA_UNITS)
                    for jj in range(4):
                        ins = nc.tensor.transpose(psum[6 + b % 2][0:keys, jj * P:(jj + 1) * P],
                                                  p_block(b)[:, jj, 0:keys], con[:, K_ID:K_ID + P])
                    ins.then_inc(pt_mm, 1)

                def outputs(b):
                    jh, n = b // 4, b % 4
                    keys = CH if n == 0 else 2 * CH
                    pe.wait_ge(pt_copied, b + 1)
                    pe.wait_ge(sw_v, 2)
                    for jj in range(4):
                        j = 4 * jh + jj
                        g = j // 2
                        if n == 2:
                            v = vmix_t[:, 0, g * 64:(g + 1) * 64]
                        else:
                            v = vt_t[0:keys, n // 2, g * 64:(g + 1) * 64]
                        for hh in range(2):
                            ins = nc.tensor.matmul(psum[j // 2][64 * hh:64 * hh + 64,
                                                                (j % 2) * T + n * CH:(j % 2) * T + (n + 1) * CH],
                                                   v, pt_block(b)[0:keys, jj, 64 * hh:64 * hh + 64],
                                                   start=True, stop=True)
                    ins.then_inc(o_mm, 1)

                proj(u, psum[0], 4, True)
                ada_reduce(ADA_SWA)
                proj_tokens(u + 1, psum[2])
                rotate(0)
                rotate(1)
                ada_reduce(ADA_SWA + 1)
                for i in range(4):
                    if i == 1:
                        pe.wait_ge(sw_evac, 2)
                    if i == 3:
                        pe.wait_ge(sw_v, 1)
                    proj(u + 2 + i, psum[(3 + i) % 4], 4, False)
                    if i:
                        rotate(1 + i)
                    if i == 0:
                        ada_reduce(ADA_SWA + 2)
                scores(0)
                rotate(5)
                scores(1)
                turn(0)
                for b in range(2, 10):
                    if b < 8:
                        scores(b)
                    if b - 1 < 8:
                        turn(b - 1)
                    outputs(b - 2)
                out_proj(u + 6, 5)

            stage_part(0)
            ffn(0)
            stage_part(1)
            hgrn()
            stage_part(2)
            ffn(1)
            stage_part(3)
            ffn(2)
            stage_part(4)
            swa()
            stage_part(5)
            ffn(3)
            stage_part(6)
            for m in range(KT):
                pe.wait_ge(hf_ready, 48 + m + 1)
                if m >= 4:
                    pe.wait_ge(out_copied, 2 * (m - 3))
                for g in range(TG):
                    ins = nc.tensor.transpose(psum[m % 4][:, g * P:(g + 1) * P], hf[:, m % 4, g * P:(g + 1) * P],
                                              con[:, K_ID:K_ID + P])
                ins.then_inc(out_t, 2)

        @block.vector
        def _(dve):
            link = [0]

            def linked(ins):
                link[0] += 1
                ins.then_inc(dve_link, 1)
                dve.wait_ge(dve_link, link[0])

            nc.vector.memset(ones[:, :], 1.0).then_inc(const_set, 1)
            nc.vector.memset(inv_d[:, :], 1.0 / D).then_inc(const_set, 1)
            nc.vector.memset(eps_t[:, :], EPS).then_inc(const_set, 1)
            dve.wait_ge(const_in, 32)
            nc.vector.tensor_copy(mask_t[:, :, :].rearrange("p a b -> p (a b)"),
                                  hf[:, 0:2, :].rearrange("p a t -> p (a t)")[:, 0:448])
            for t, (dst, n) in enumerate(((adab[:, 0:72], 72), (adab[:, 72:144], 72), (vec[:, :], C_ROWS))):
                dve.wait_ge(stage_t, 3)
                nc.vector.tensor_copy(dst, psum[4][:, t * P:t * P + n]).then_inc(vec_ready, 1)
            dve.wait_ge(vec_ready, 3)
            lbr = vec[:, C_LB:C_LB + 24].rearrange("p (l a) -> p l a", l=3)
            linked(nc.vector.tensor_tensor(small[:, 3, :], lbr[:, 0, :], lbr[:, 1, :], ALU.max))
            linked(nc.vector.tensor_tensor(small[:, 3, :], small[:, 3, :], lbr[:, 2, :], ALU.max))
            for r in range(3):
                nc.vector.tensor_tensor(small[:, r, :], lbr[:, r, :], small[:, 3, :], ALU.subtract)\
                    .then_inc(const_set, 1)
            dve.wait_ge(const_set, 6)
            dve.wait_ge(x_in, 16 * 4)
            for t in range(2):
                half = slice(64 * t, 64 * t + 64)
                linked(nc.vector.tensor_copy(sink[half, :],
                                             sink_all[half, :].rearrange("p (j t) -> p t j", t=2)[:, t, :]))
            linked(nc.vector.tensor_copy(cosb[:, :], sinb[:, :].bitcast(I32)))
            linked(nc.vector.tensor_scalar(xr[:, 0, :], cosb[:, :], con[:, K_FREQ:K_FREQ + 1], None, ALU.mult))
            linked(nc.vector.tensor_scalar(xr[:, 1, :], xr[:, 0, :], float(0.5 / np.pi), MAGIC, ALU.mult, ALU.add))
            linked(nc.vector.tensor_scalar(xr[:, 1, :], xr[:, 1, :], MAGIC, None, ALU.subtract))
            parts = (6.28125, 0.0019340515136718750, float(2 * np.pi - 6.28125 - 0.0019340515136718750))
            for part in parts:
                linked(nc.vector.scalar_tensor_tensor(out=xr[:, 0, :], in0=xr[:, 1, :], scalar=-part,
                                                      in1=xr[:, 0, :], op0=ALU.mult, op1=ALU.add))
            linked(nc.vector.tensor_scalar(xr[:, 1, :], xr[:, 0, :], 3.1415925, -3.1415925, ALU.min, ALU.max))
            linked(nc.vector.tensor_scalar(xr[:, 0, :], xr[:, 1, :], -1.0, None, ALU.mult))
            linked(nc.vector.tensor_tensor(xr[:, 0, :], xr[:, 0, :], xr[:, 1, :], ALU.min))
            nc.vector.tensor_scalar(xr[:, 0, :], xr[:, 0, :], float(np.pi / 2), None, ALU.add).then_inc(angle, 1)

            def ada_steps(a, step=0, i=0):
                slot = a % 2
                w = ada_raw[:, slot, :].rearrange("p (k c) -> p k c", k=KT)

                def one(k):
                    if k == 0:
                        if step == 4:
                            dve.wait_ge(ada_landed[slot], 16 * (a // 2 + 1) + 32 * i)
                        else:
                            dve.wait_ge(ada_landed[slot], 16 * (a // 2 + 1) + 16 * i)
                        nc.vector.tensor_scalar(acc[:, :], w[:, 0, :], c_act[:, 0:1], None, ALU.mult)\
                            .then_inc(ada_step, 1)
                        return
                    dve.wait_ge(ada_step, 8 * a + 8 * step * i + k)
                    nc.vector.scalar_tensor_tensor(out=acc[:, :], in0=w[:, k, :], scalar=c_act[:, k:k + 1],
                                                   in1=acc[:, :], op0=ALU.mult, op1=ALU.add).then_inc(ada_step, 1)
                return one

            def ada_finish(a, step=0, i=0):
                dve.wait_ge(ada_sum, a + step * i + 1)
                col = 2 * (a % 2)
                at = bass.ds(2 * a + 2 * step * i, 2)
                nc.vector.tensor_tensor(adac[:, at], psum[ADA_BANK][:, col:col + 2], adab[:, at], ALU.add)\
                    .then_inc(ada_out, 1)

            dve.wait_ge(c_ready, 1)
            for a in range(ADA_START):
                one = ada_steps(a)
                for k in range(KT):
                    one(k)
                ada_finish(a)
            dve.wait_ge(c_ready, 2)
            linked(nc.vector.tensor_tensor(small[:, 3, :], small[:, 0, :], small[:, 1, :], ALU.add))
            linked(nc.vector.tensor_tensor(small[:, 3, :], small[:, 3, :], small[:, 2, :], ALU.add))
            linked(nc.vector.reciprocal(small[:, 4, :], small[:, 3, :]))
            linked(nc.vector.tensor_tensor(lb[:, :], small[:, 0, :], small[:, 4, :], ALU.mult))
            linked(nc.vector.tensor_scalar(oml[:, :], lb[:, :], -1.0, 1.0, ALU.mult, ALU.add))
            dve.wait_ge(c_ready, 4)

            ADA_NEEDED = [8, 20, 30, 44, 58, 72, 72]

            def stage_part(b):
                if b < 6:
                    for j in first_jobs(b):
                        split_lo(dve, *j)
                ADA_DONE = {0: 8, 1: 30, 2: 36, 3: 58, 4: 69, 5: 72, 6: 72}[b]
                dve.wait_ge(ada_out, ADA_DONE)
                if b:
                    r = b - 1
                    gc = (r // 3) * 72 + 24 * (r % 3) + 16
                    linked(nc.vector.tensor_scalar(gcol[:, :], adac[:, gc:gc + KT], 1.0 if r % 3 == 1 else 0.5,
                                                   None, ALU.mult))
                if b < 6:
                    sc = (b // 3) * 72 + 24 * (b % 3) + 8
                    ng = C_NORM + 8 * b
                    nc.vector.scalar_tensor_tensor(out=scol[:, :], in0=adac[:, sc:sc + KT], scalar=1.0,
                                                   in1=vec[:, ng:ng + KT], op0=ALU.add, op1=ALU.mult)\
                        .then_inc(cols_ready, 1)
                else:
                    nc.vector.tensor_copy(scol[:, :], vec[:, C_FINAL:C_FINAL + KT]).then_inc(cols_ready, 1)
                if b == 5:
                    linked(nc.vector.tensor_tensor(small[:, 5, :], gcol[:, :], vec[:, C_BO:C_BO + KT], ALU.mult))
                for m in range(KT):
                    y_wait(dve, b, m)
                    if b == 0:
                        nc.vector.tensor_copy(xT[:, m, :], y_acc(m)).then_inc(x_ready, 1)
                        continue
                    y = y_pair(m) if b in (2, 5) else y_acc(m)
                    if b == 5:
                        linked(nc.vector.tensor_scalar(xT[:, m, :], xT[:, m, :], small[:, 5, m:m + 1], None,
                                                       ALU.add))
                    nc.vector.scalar_tensor_tensor(out=xT[:, m, :], in0=y, scalar=gcol[:, m:m + 1],
                                                   in1=xT[:, m, :], op0=ALU.mult, op1=ALU.add).then_inc(x_ready, 1)
                dve.wait_ge(x_ready, 8 * b + 8)
                dve.wait_ge(sd_ready, b + 1)
                linked(nc.vector.reciprocal(rstd[:, :], sd[:, :]))
                for m in range(KT + 1):
                    g = 8 * b + m
                    if m < KT:
                        if m >= 4:
                            dve.wait_ge(hf_ready, g - 3)
                        nc.vector.tensor_tensor(xr[:, m % 4, :], xT[:, m, :], rstd[:, :], ALU.mult)\
                            .then_inc(xr_ready, 1)
                    if m and b < 6:
                        dve.wait_ge(h_hi_ready, g)
                        nc.vector.tensor_tensor(h_lo[:, m - 1, :], hf[:, (m - 1) % 4, :],
                                                h_hi[:, m - 1, :].bitcast(F32), ALU.subtract)\
                            .then_inc(h_lo_ready, 1)

            def ffn_half(n, it, hf_, i=0):
                jobs = half_jobs(n, it, hf_)
                a, step = ada_of(n, it, hf_)
                one = ada_steps(a, step, i) if a is not None else None
                for t in range(4):
                    if t < len(jobs):
                        split_lo(dve, *jobs[t], i=i)
                    if one:
                        one(2 * t)
                        one(2 * t + 1)
                g = NF * n + 2 * it + hf_
                dve.wait_ge(silu_done, g + 4 * i + 1)
                nc.vector.tensor_tensor(act_f[:, hf_, :], sil[:, hf_, :], psum[4 + hf_][:, T:2 * T], ALU.mult)\
                    .then_inc(a_mul, 1)
                dve.wait_ge(a_hi_ready, g + 4 * i + 1)
                nc.vector.tensor_tensor(a_lo[:, hf_, :], act_f[:, hf_, :], a_hi[:, hf_, :].bitcast(F32),
                                        ALU.subtract).then_inc(a_lo_ready, 1)
                if one:
                    ada_finish(a, step, i)

            def ffn(n):
                for hf_ in range(2):
                    ffn_half(n, 0, hf_)
                with dve.Fori(0, (NIT - 3) // 2) as i:
                    for it in (1, 2):
                        for hf_ in range(2):
                            ffn_half(n, it, hf_, i)
                for it in (NIT - 2, NIT - 1):
                    for hf_ in range(2):
                        ffn_half(n, it, hf_)

            def halves(ap, h):
                v = ap.rearrange("p a (n b h) -> p a n b h", b=2, h=h)
                return v[:, :, :, 0, :], v[:, :, :, 1, :]

            def hgrn():
                u = UNIT_BASE["hgrn"]
                def proj_evac(w):
                    if w < 12 and w % 3 == 2:
                        return
                    dve.wait_ge(proj_read, w + 1)
                    p = w // 3 if w < 12 else w - 12
                    if w < 12 and p >= 2:
                        dve.wait_ge(chain_mm, STEP_AT[(p - 2, 7)] + 1)
                    if w >= 12:
                        ins = nc.vector.tensor_tensor(mix[:, 2 * p:2 * p + 2, :], mix[:, 2 * p:2 * p + 2, :],
                                                      sg_t[0][:, :, :], ALU.mult)
                    elif w % 3 == 0:
                        ins = nc.vector.tensor_tensor(q_t[p % 2][:, :, :], sg_t[0][:, :, :], sg_t[1][:, :, :],
                                                      ALU.mult)
                    else:
                        for hh in range(2):
                            j = 2 * p + hh
                            nc.vector.tensor_scalar(f_t[p % 2][:, hh, :], sg_t[0][:, hh, :],
                                                    oml[:, j:j + 1], lb[:, j:j + 1], ALU.mult, ALU.add)
                        for hh in range(2):
                            j = 2 * p + hh
                            ins = nc.vector.tensor_scalar(k_t[p % 2][:, hh, :], sg_t[1][:, hh, :],
                                                          oml[:, j:j + 1], None, ALU.mult)
                    ins.then_inc(gates_used, 1)

                def make(c_, p, s):
                    q, k, f = q_t[p % 2], k_t[p % 2], f_t[p % 2]
                    if s == "D":
                        dve.wait_ge(gates_used, 2 * p + 2)
                        for b_ in range(2):
                            if p == 0:
                                nc.vector.tensor_copy(kl_t[b_][:, :, :], k[:, :, :])
                        linked(nc.vector.memset(r_t[:, :, :], 1.0))
                        return
                    h = 1 << s
                    fl, fr = halves(f[:, :, :], h)
                    rl, _ = halves(r_t[:, :, :], h)
                    if s >= 2 or p:
                        before = STEP_AT[(p, s - 2)] if s >= 2 else STEP_AT[(p - 1, 6 + s)]
                        dve.wait_ge(chain_mm, before + 1)
                    ins = nc.vector.tensor_tensor(
                        ql_view(s).rearrange("p a (n h) -> p a n h", h=h), halves(q[:, :, :], h)[1], fr, ALU.mult)
                    if s:
                        ins = nc.vector.tensor_tensor(halves(kl_t[s % 2][:, :, :], h)[0],
                                                      halves(k[:, :, :], h)[0], rl, ALU.mult)
                    ins.then_inc(chain_in, 1)
                    if s < LEVELS - 1:
                        n = T // (2 * h)
                        shape = [P, 2, n, h]
                        linked(nc.vector.tensor_tensor(rl, rl, fr[:, :, :, h - 1:h].broadcast_to(shape), ALU.mult))
                        linked(nc.vector.tensor_tensor(fr, fr, fl[:, :, :, h - 1:h].broadcast_to(shape), ALU.mult))

                def take(c_, p, s):
                    if s in ("O", "S"):
                        return
                    dve.wait_ge(chain_mm, c_ + 1)
                    bank = chain_bank(c_)
                    at = at_t[p % 2]
                    if s == "D":
                        if p >= 2:
                            dve.wait_ge(chain_mm, STEP_AT[(p - 2, "O")] + 1)
                        eye = con[:, K_ID:K_ID + P].unsqueeze(1).broadcast_to([P, 4, P])
                        ins = nc.vector.tensor_tensor(at[:, :, :].rearrange("p a (g t) -> p (a g) t", g=TG),
                                                      bank.rearrange("p a (g t) -> p (a g) t", g=TG), eye, ALU.mult)
                    elif s == 7:
                        ins = nc.vector.tensor_copy(at2_t[:, p % 2, :, :],
                                                    bank[:, 0, :].rearrange("p (a t) -> p a t", a=2))
                    else:
                        h = 1 << s
                        n = 64 // h
                        dst = at[:, :, :].rearrange("p a (g t) -> p (a g) t", g=TG)\
                            .rearrange("p q (n b h) -> p q n b h", b=2, h=h)[:, :, :, 1, :]
                        m = mask_t[:, s, :].rearrange("p (n h) -> p n h", h=h).unsqueeze(1)\
                            .broadcast_to([P, 4, n, h])
                        data = bank[:, 0, :].rearrange("p (q n h) -> p q n h", q=4, h=h)
                        dve.wait_ge(chain_read_dve, taken[0])
                        ins = nc.vector.copy_predicated(dst, m, data)
                    ins.then_inc(chain_read_dve, 1)
                    taken[0] += 1

                taken = [0]

                def normed(p):
                    dve.wait_ge(osd_ready, p + 1)
                    linked(nc.vector.reciprocal(osd_t[:, :, :], osd_t[:, :, :]))
                    for hh in range(2):
                        j = 2 * p + hh
                        ins = nc.vector.scalar_tensor_tensor(out=mix[:, j, :], in0=o_t[:, hh, :],
                                                             scalar=vec[:, C_HGN + j:C_HGN + j + 1],
                                                             in1=osd_t[:, hh, :], op0=ALU.mult, op1=ALU.mult)
                        if hh == 0:
                            linked(ins)
                    ins.then_inc(o_normed, 1)
                    dve.wait_ge(o_normed, p + 1)

                for w in range(19):
                    if w < 17:
                        for j in unit_jobs(u + w + 1):
                            split_lo(dve, *j)
                    one = None
                    if w in HG_ADA:
                        a = ADA_HGRN + HG_ADA.index(w)
                        one = ada_steps(a)
                        for k in range(KT):
                            one(k)
                    if 1 <= w <= 15:
                        proj_evac(w - 1)
                    for c_, (ws, p, s) in enumerate(STEPS):
                        if ws == w - 1:
                            take(c_, p, s)
                            if s == "S":
                                normed(p)
                    if w == 18:
                        proj_evac(15)
                    for c_, (ws, p, s) in enumerate(STEPS):
                        if ws == w and s not in ("O", "S"):
                            make(c_, p, s)
                    if one:
                        ada_finish(a)
                for p in range(NP_HG):
                    dve.wait_ge(mix_hi, p + 1)
                    nc.vector.tensor_tensor(h_lo[:, 2 * p:2 * p + 2, :], mix[:, 2 * p:2 * p + 2, :],
                                            h_hi[:, 2 * p:2 * p + 2, :].bitcast(F32), ALU.subtract)\
                        .then_inc(mix_lo, 1)
                for w in range(18, 20):
                    for j in unit_jobs(u + w):
                        split_lo(dve, *j)

            def swa():
                u = UNIT_BASE["swa"]

                def rope(r):
                    src = psum[4 + RING_AT[("C", r)] % 2][:, :].rearrange("p (a t) -> p a t", a=2) if r < 2 \
                        else raw_t[(r - 1) % 2]
                    dst = rk_t[r] if r < 2 else rq_t[r - 2]
                    cb = cosb[:, :].unsqueeze(1).broadcast_to([P, 2, T])
                    sb_ = sinb[:, :].unsqueeze(1).broadcast_to([P, 2, T])
                    dve.wait_ge(rope_mm, r + 1)
                    if r:
                        dve.wait_ge(rope_done, r)
                    nc.vector.tensor_tensor(rope_t[0][:, :, :], src[:, :, :], cb, ALU.mult)
                    linked(nc.vector.tensor_tensor(
                        rope_t[1][:, :, :], psum[r_bank(r)][:, :].rearrange("p (a t) -> p a t", a=2), sb_, ALU.mult))
                    nc.vector.tensor_tensor(dst[:, :, :], rope_t[0][:, :, :], rope_t[1][:, :, :], ALU.add)\
                        .then_inc(rope_done, 1)

                def evac_v():
                    dve.wait_ge(w_used, 2 * (u + 2))
                    nc.vector.tensor_tensor(
                        vt_t[:, :, :], psum[2][:, :].rearrange("p (a t) -> p a t", a=2),
                        bv[:, :].unsqueeze(1).broadcast_to([P, 2, T]), ALU.add).then_inc(sw_v, 1)
                    dve.wait_ge(sw_v, 1)
                    nc.vector.tensor_copy(vmix_t[0:64, 0, :], vt_t[0:64, 1, :])
                    nc.vector.tensor_copy(vmix_t[64:P, 0, :], vt_t[64:P, 0, :]).then_inc(sw_v, 1)

                def bound(b):
                    jh, n = b // 4, b % 4
                    keys = CH if n == 0 else 2 * CH
                    st = stat[:, b % 2, :, :]
                    dve.wait_ge(s_mm, b + 1)
                    if b >= 2:
                        dve.wait_ge(p_exp, 5 * (b - 1))
                    snk = sink[:, 4 * jh:4 * jh + 4]
                    linked(nc.vector.tensor_reduce(
                        st[:, 0, :], psum[s_bank(b)][:, :].rearrange("p (j t) -> p j t", j=4)[:, :, 0:keys], AX,
                        ALU.max))
                    linked(nc.vector.scalar_tensor_tensor(out=st[:, 1, :], in0=st[:, 0, :], scalar=0.125, in1=snk,
                                                          op0=ALU.mult, op1=ALU.max))
                    nc.vector.tensor_scalar(st[:, 2, :], st[:, 1, :], -1.0, None, ALU.mult)
                    nc.vector.tensor_tensor(st[:, 3, :], snk, st[:, 1, :], ALU.subtract).then_inc(s_max, 1)

                def norm(b):
                    keys = CH if b % 4 == 0 else 2 * CH
                    st = stat[:, b % 2, :, :]
                    dve.wait_ge(p_exp, 5 * (b + 1))
                    linked(nc.vector.tensor_tensor(st[:, 6, :], st[:, 4, :], st[:, 5, :], ALU.add))
                    linked(nc.vector.reciprocal(st[:, 7, :], st[:, 6, :]))
                    blk = p_block(b)[:, :, 0:keys]
                    nc.vector.tensor_tensor(blk, blk, st[:, 7, :].unsqueeze(2).broadcast_to([P, 4, keys]), ALU.mult)\
                        .then_inc(p_norm, 1)

                for w in range(7):
                    if w + 1 < 8:
                        for j in unit_jobs(u + w + 1):
                            split_lo(dve, *j)
                    if w < 3:
                        one = ada_steps(ADA_SWA + w)
                        for k in range(KT):
                            one(k)
                        if w == 1:
                            rope(0)
                            evac_v()
                            rope(1)
                        ada_finish(ADA_SWA + w)
                    if w >= 4:
                        rope(w - 2)
                bound(0)
                rope(5)
                bound(1)
                norm(0)
                for b in range(2, 9):
                    if b < 8:
                        bound(b)
                    norm(b - 1)
                    if b == 6:
                        for jp in range(2):
                            o_lo(jp)
                for jp in range(2, 4):
                    o_lo(jp)
                for w in range(8, 10):
                    for j in unit_jobs(u + w):
                        split_lo(dve, *j)

            def o_lo(jp):
                dve.wait_ge(mix_hi, 4 + jp + 1)
                nc.vector.tensor_tensor(h_lo[:, 2 * jp:2 * jp + 2, :], psum[jp][:, :].rearrange("p (a t) -> p a t", a=2),
                                        h_hi[:, 2 * jp:2 * jp + 2, :].bitcast(F32), ALU.subtract).then_inc(mix_lo, 1)

            stage_part(0)
            ffn(0)
            stage_part(1)
            hgrn()
            stage_part(2)
            ffn(1)
            stage_part(3)
            ffn(2)
            stage_part(4)
            swa()
            stage_part(5)
            ffn(3)
            stage_part(6)


_INS = ["x", "c", "positions", "ada_w", "ada_b", "norm_g", "ffn1_w_gu", "ffn1_w_down", "ffn2_w_gu", "ffn2_w_down",
        "hg_w_in", "hg_lower_bounds", "hg_norm_g", "hg_w_out", "sw_w_qkv", "sw_b_qkv", "sw_sinks", "sw_w_out",
        "sw_b_out", "final_norm_g"]


def kernel(**inputs):
    import concourse.bacc as _bacc
    from concourse import mybir as _mybir
    from concourse.bass_utils import run_bass_kernel_spmd as _run

    nc = _bacc.Bacc("TRN2", target_bir_lowering=False, num_devices=1)
    arrays, args = {}, []
    for name, a in [(n, inputs[n]) for n in _INS] + list(zip(("consts", "masks"), constants())):
        a = np.ascontiguousarray(a)
        arrays[f"in_{name}_dram"] = a
        args.append(nc.dram_tensor(f"in_{name}_dram", a.shape, _mybir.dt.from_np(a.dtype), kind="ExternalInput").ap())
    out = nc.dram_tensor("out_dram", (1, T, D), _mybir.dt.float32, kind="ExternalOutput").ap()
    trunk(nc, *args, out)
    r = _run(nc, [arrays], core_ids=[0])
    return r.results[0]["out_dram"]
```

```python
from contextlib import ExitStack

import numpy as np
import concourse.bass as bass
from concourse import mybir

ALU = mybir.AluOpType
ACT = mybir.ActivationFunctionType
AX = mybir.AxisListType.X
F32 = mybir.dt.float32
F32R = mybir.dt.float32r
I32 = mybir.dt.int32
U8 = mybir.dt.uint8

P = 128
D = 1024
T = 256
KT = D // P
TG = T // P
DFF = 2816
NF = DFF // P
NIT = NF // 2
UNIT = 2048
HALF = UNIT // 2
RAW = 6
JOBS = 6
EPS = 1e-6
CH = 64
NP_HG = 4
LEVELS = 8
HALF_ROPE = 8
MAGIC = 12582912.0

FFN_UNITS = 3 * NIT
UNIT_BASE = {"ffn0": 0}
UNIT_BASE["hgrn"] = UNIT_BASE["ffn0"] + FFN_UNITS
UNIT_BASE["ffn1"] = UNIT_BASE["hgrn"] + 20
UNIT_BASE["ffn2"] = UNIT_BASE["ffn1"] + FFN_UNITS
UNIT_BASE["swa"] = UNIT_BASE["ffn2"] + FFN_UNITS
UNIT_BASE["ffn3"] = UNIT_BASE["swa"] + 10
ADA_PE = 4
ADA_START = 8
ADA_FFN = {0: (8, 2), 1: (32, 2), 2: (54, 1)}
ADA_HGRN = 30
HG_ADA = [1, 2]
ADA_SWA = 65
ADA_LAST = 69
ADA_NEEDED = [8, 20, 32, 44, 56, 68, 72]

C_NORM, C_FINAL, C_LB, C_HGN, C_BQ, C_BO, C_C, C_ROWS = 0, 48, 56, 80, 88, 98, 106, 114
K_ID, K_PERM, K_DUP, K_FREQ, K_COLS = 0, 128, 256, 768, 769


def constants():
    k = np.zeros((P, K_COLS), np.float32)
    masks = np.zeros((P, 7 * 64), np.float32)
    for t in range(2):
        for p in range(P):
            k[64 * t + p % 64, K_DUP + t * P + p] = 1.0
    k[:, K_ID:K_ID + P] = np.eye(P, dtype=np.float32)
    for p in range(P):
        r = p % 64
        if r < HALF_ROPE:
            k[p + HALF_ROPE, K_PERM + p] = -1.0
        elif r < 2 * HALF_ROPE:
            k[p - HALF_ROPE, K_PERM + p] = 1.0
        if r < 2 * HALF_ROPE:
            for t in range(2):
                sign, at = (-1.0, r + HALF_ROPE) if r < HALF_ROPE else (1.0, r - HALF_ROPE)
                k[64 * t + at, K_DUP + (2 + t) * P + p] = sign
            k[p, K_FREQ] = np.float32(500000.0) ** (-np.float32(r % HALF_ROPE) / np.float32(HALF_ROPE))
    for lev in range(7):
        h = 1 << lev
        for s in range(P):
            if (s // h) % 2 == 0:
                n = s // (2 * h)
                masks[s, 64 * lev + n * h:64 * lev + (n + 1) * h] = 1.0
    return k, masks


def ffn_job(it, what, last=NIT - 1):
    if what == "G0":
        return 6 * it - 1 if it else 0
    if what == "U0":
        return 6 * it if it else 1
    if what == "D1":
        return 6 * it + (5 if it == last else 7)
    return 6 * it + {"G1": 2, "U1": 3, "D0": 4}[what]


def hgrn_steps():
    out = []
    for w in range(18):
        if w >= 6 and (w - 6) % 3 == 0:
            out.append((w, (w - 6) // 3, "O"))
        if w >= 7 and (w - 7) % 3 == 0 and (w - 7) // 3 < NP_HG:
            out.append((w, (w - 7) // 3, "S"))
        if w >= 8 and (w - 8) % 3 == 0:
            out.append((w, (w - 8) // 3, "B"))
        if 3 <= w < 15:
            p, g = (w - 3) // 3, (w - 3) % 3
            out += [(w, p, s) for s in (["D", 0, 1], [2, 3, 4], [5, 6, 7])[g]]
    return out


def trunk(nc, x, c, positions, ada_w, ada_b, norm_g, ffn1_w_gu, ffn1_w_down, ffn2_w_gu, ffn2_w_down,
          hg_w_in, hg_lower_bounds, hg_norm_g, hg_w_out, sw_w_qkv, sw_b_qkv, sw_sinks, sw_w_out,
          sw_b_out, final_norm_g, consts, masks, out):
    STEPS = hgrn_steps()
    STEP_AT = {(p, s): i for i, (_, p, s) in enumerate(STEPS)}

    with ExitStack() as ctx:
        def sb(name, shape, dt=F32):
            return ctx.enter_context(nc.sbuf_tensor(name, shape, dt))

        def sem(name):
            return ctx.enter_context(nc.semaphore(name))

        raw = sb("raw", [P, RAW, UNIT])
        ada_raw = sb("ada_raw", [P, 2, UNIT])
        w_hi = sb("w_hi", [P, JOBS, HALF], F32R)
        w_lo = sb("w_lo", [P, JOBS, HALF], F32R)
        xT = sb("xT", [P, KT, T])
        h_hi = sb("h_hi", [P, KT, T], F32R)
        h_lo = sb("h_lo", [P, KT, T], F32R)
        mix = sb("mix", [P, KT, T])
        sq = sb("sq", [P, 4, T])
        xr = sb("xr", [P, 4, T])
        hf = sb("hf", [P, 4, T])
        sd = sb("sd", [P, T])
        rstd = sb("rstd", [P, T])
        ffn_f = sb("ffn_f", [P, 4, T])
        sil, act_f = ffn_f[:, 0:2, :], ffn_f[:, 2:4, :]
        ada_row = ffn_f[0:1, :, :]
        a_hi = sb("a_hi", [P, 2, T], F32R)
        a_lo = sb("a_lo", [P, 2, T], F32R)
        acc = sb("acc", [P, 2, T])
        con = sb("con", [P, K_COLS])
        mask_t = sb("mask_t", [P, 7, 64], U8)
        ones = sb("ones", [P, P])
        inv_d = sb("inv_d", [P, P])
        eps_t = sb("eps_t", [P, 1])
        warm = sb("warm", [P, 1])
        stage = sb("stage", [P, 3, P])
        adab = sb("adab", [P, 144])
        adac = sb("adac", [P, 144])
        vec = sb("vec", [P, C_ROWS])
        c_act = sb("c_act", [P, KT])
        osd = sb("osd", [P, 2 * TG])
        orstd = sb("orstd", [P, 2 * TG])
        scol = sb("scol", [P, KT])
        gcol = sb("gcol", [P, KT])
        small = sb("small", [P, 8, KT])
        lb = sb("lb", [P, KT])
        oml = sb("oml", [P, KT])
        sink = sb("sink", [P, KT])
        sink_all = sb("sink_all", [P, 2 * KT])
        bv = sb("bv", [P, T])
        cosb = sb("cosb", [P, T])
        sinb = sb("sinb", [P, T])
        shared = [v for tile_ in (sq, xr, hf) for v in (tile_[:, 0:2, :], tile_[:, 2:4, :])]
        m512 = shared + [sb(f"m512_{i}", [P, 2, T]) for i in range(11)]
        at_0 = sb("at_0", [P, 4, T])
        stat = sb("stat", [P, 2, 8, 4])

        psum = [ctx.enter_context(nc.psum_tensor(f"bank{i}", [P, 512], F32)) for i in range(8)]
        SUMS, ADA_BANK = 7, 6

        def y_acc(m):
            return psum[m // 2][:, (m % 2) * T:(m % 2 + 1) * T]

        raw_landed = [sem(f"raw_landed{i}") for i in range(RAW)]
        ada_landed = [sem(f"ada_landed{i}") for i in range(2)]
        w_hi_ready = sem("w_hi_ready")
        w_lo_ready = sem("w_lo_ready")
        w_used = sem("w_used")
        ada_step = sem("ada_step")
        ada_sum = sem("ada_sum")
        ada_out = sem("ada_out")
        ada_pe = sem("ada_pe")
        ada_row_read = sem("ada_row_read")
        ada_turned = sem("ada_turned")
        small_in = sem("small_in")
        x_in = sem("x_in")
        const_in = sem("const_in")
        const_set = sem("const_set")
        stage_t = sem("stage_t")
        vec_ready = sem("vec_ready")
        c_ready = sem("c_ready")
        dve_link = sem("dve_link")
        act_link = sem("act_link")
        angle = sem("angle")
        y_done = sem("y_done")
        x_ready = sem("x_ready")
        sq_ready = sem("sq_ready")
        sq_pair = sem("sq_pair")
        ss_done = sem("ss_done")
        sd_ready = sem("sd_ready")
        xr_ready = sem("xr_ready")
        cols_ready = sem("cols_ready")
        hf_ready = sem("hf_ready")
        h_lo_ready = sem("h_lo_ready")
        silu_done = sem("silu_done")
        a_mul = sem("a_mul")
        a_hi_ready = sem("a_hi_ready")
        a_lo_ready = sem("a_lo_ready")
        proj_read = sem("proj_read")
        gates_used = sem("gates_used")
        fk_ready = sem("fk_ready")
        lb_ready = sem("lb_ready")
        chain_in = sem("chain_in")
        chain_mm = sem("chain_mm")
        chain_read_dve = sem("chain_read_dve")
        osq_ready = sem("osq_ready")
        osd_ready = sem("osd_ready")
        orstd_ready = sem("orstd_ready")
        o_normed = sem("o_normed")
        mix_hi = sem("mix_hi")
        mix_lo = sem("mix_lo")
        sw_evac = sem("sw_evac")
        sw_v = sem("sw_v")
        k_mixed = sem("k_mixed")
        rope_mm = sem("rope_mm")
        rope_done = sem("rope_done")
        s_half = sem("s_half")
        s_mm = sem("s_mm")
        s_max = sem("s_max")
        p_exp = sem("p_exp")
        p_norm = sem("p_norm")
        pt_mm = sem("pt_mm")
        pt_copied = sem("pt_copied")
        o_mm = sem("o_mm")
        out_t = sem("out_t")
        out_copied = sem("out_copied")
        stored = sem("stored")

        def cols(w, c0, n=256):
            return w.rearrange("(k p) c -> p k c", p=P)[:, :, bass.ds(c0, n)]

        GU = [ffn1_w_gu[0], ffn2_w_gu[0], ffn1_w_gu[1], ffn2_w_gu[1]]
        DOWN = [ffn1_w_down[0], ffn2_w_down[0], ffn1_w_down[1], ffn2_w_down[1]]
        HG_COL = [(w // 3) * 256 + (w % 3) * D if w < 12 else 3 * D + (w - 12) * 256 for w in range(16)]
        SW_COL = [D, D + 256, 0, 256, 512, 768]
        POST = {0: "ffn0", 1: "hgrn", 2: "ffn1", 3: "ffn2", 4: "swa", 5: "ffn3"}

        def gu_count(n, it, hf_):
            return 2 * UNIT_BASE[f"ffn{n}"] + ffn_job(it, f"G{hf_}") + 2

        def down_count(n, it, hf_):
            return 2 * UNIT_BASE[f"ffn{n}"] + ffn_job(it, f"D{hf_}") + 1

        def split_count(unit):
            for n in range(4):
                u = UNIT_BASE[f"ffn{n}"]
                if u <= unit < u + FFN_UNITS:
                    it, r = divmod(unit - u, 3)
                    return 2 * u + ffn_job(it, ("G1", "U1", "D1")[r]) + 1
            return 2 * unit + 2

        Y_STAGES = [0, 1, 3, 4, 6]

        def y_wait(eng, b, m):
            m |= 1
            if b in (2, 5):
                eng.wait_ge(w_used, 2 * (UNIT_BASE["hgrn"] + 16 if b == 2 else UNIT_BASE["swa"] + 6) + m + 1)
            else:
                eng.wait_ge(y_done, 8 * Y_STAGES.index(b) + m + 1)

        def ada_place(a):
            if a < ADA_START and a not in (ADA_PE, ADA_PE + 1):
                slot = a if a < ADA_PE else a - 2
                return raw[:, slot, :], raw_landed[slot]
            return ada_raw[:, a % 2, :], ada_landed[a % 2]

        def ada_turn(a):
            return 1 if a < ADA_START else (a - ADA_START) // 2 + 2

        def made(a):
            return a - ADA_PE

        def square(m):
            return sq[:, m, :] if m < 4 else hf[:, m - 4, :]

        ROW_BANK = (4, 1, 2, 3)

        def raw_cols(slot):
            return raw[:, slot, :].rearrange("p (k c) -> p k c", k=KT)

        def even(u, i):
            return u % RAW, u // RAW + 1 + i

        block = ctx.enter_context(nc.Block())

        @block.sync
        def _(sp):
            def load_unit(u, src, i=0, k=KT, free_at=None):
                slot, turn = even(u, i)
                if u < RAW:
                    if u < ADA_PE:
                        sp.wait_ge(ada_pe, u + 1)
                    else:
                        sp.wait_ge(ada_step, 8 * made(u + 2) + 8)
                else:
                    sp.wait_ge(w_lo_ready, free_at + 12 * i if free_at is not None else split_count(u - RAW))
                sp.dma_start(raw[:, slot, :].rearrange("p (k c) -> p k c", k=k), src).then_inc(raw_landed[slot], 16)

            def load_ada(a, i=0, per=0):
                if a < ADA_START:
                    dst, landed = ada_place(a)
                else:
                    before = a - 2 if a >= ADA_START + 2 else a - 4
                    sp.wait_ge(ada_step, 8 * made(before) + 8 + 8 * per * i)
                    dst, landed = ada_raw[:, a % 2, :], ada_landed[a % 2]
                src = cols(ada_w[a // 36], (a % 36) * 256 + i * 256 * per)
                sp.dma_start(dst.rearrange("p (k c) -> p k c", k=KT), src).then_inc(landed, 16)

            sp.dma_start(con[:, :], consts).then_inc(const_in, 16)
            sp.dma_start(hf[:, 0:2, :].rearrange("p a t -> p (a t)")[:, 0:448], masks).then_inc(const_in, 16)
            for layer in range(2):
                sp.dma_start(stage[0:72, layer, :], ada_b[layer].rearrange("(a b) -> a b", b=P)).then_inc(small_in, 16)
            rows = [(C_NORM, norm_g.rearrange("l s (a b) -> (l s a) b", b=P)),
                    (C_FINAL, final_norm_g.rearrange("(a b) -> a b", b=P)),
                    (C_LB, hg_lower_bounds.rearrange("l (a b) -> (l a) b", b=P)),
                    (C_HGN, hg_norm_g[0].rearrange("(a b) -> a b", b=P)),
                    (C_BQ, sw_b_qkv[0, 0:D + 256].rearrange("(a b) -> a b", b=P)),
                    (C_BO, sw_b_out[0].rearrange("(a b) -> a b", b=P)),
                    (C_C, c[0].rearrange("(a b) -> a b", b=P))]
            for r, src in rows:
                sp.dma_start(stage[r:r + src.shape[0], 2, :], src).then_inc(small_in, 16)
            sp.dma_start(mix[:, :, :].rearrange("p (g a) t -> p g (a t)", g=TG),
                         x[0].rearrange("(g p) d -> p g d", p=P)).then_inc(x_in, 16)
            pos = positions[0:1, :].broadcast_to([P, T])
            sp.dma_start(sinb[:, :].bitcast(I32), pos).then_inc(x_in, 16)
            sp.dma_start(bv[:, :], sw_b_qkv[0:1, D + 256:D + 512].broadcast_to([P, T])).then_inc(x_in, 16)
            sp.dma_start(sink_all[:, :], sw_sinks.broadcast_to([P, 2 * KT])).then_inc(x_in, 16)
            for a in range(ADA_PE):
                load_ada(a)
                load_ada(ADA_PE + a)

            def ada_behind(n, it, i=0):
                if n == 3:
                    return [None, None]
                ada0, per = ADA_FFN[n]
                units = [(ada0 + per * it + t, i, 2 * per) for t in range(per)]
                return units + [None] * (2 - per)

            def ffn_loads(n, it, i=0):
                u = UNIT_BASE[f"ffn{n}"] + 3 * it
                free = [2 * UNIT_BASE[f"ffn{n}"] + 6 * (it - 2) + j + 1 for j in (2, 3, 7)] if it >= 2 else [None] * 3
                c0 = it * 256 + i * 512
                ada = ada_behind(n, it - 1, i) if it else behind
                load_unit(u, cols(GU[n], c0), i, free_at=free[0])
                load_unit(u + 1, cols(GU[n], c0 + DFF), i, free_at=free[1])
                if ada[0]:
                    load_ada(*ada[0])
                load_unit(u + 2, DOWN[n].rearrange("(a p) c -> p a c", p=P)[:, bass.ds(2 * it + 4 * i, 2), :], i, 2,
                          free_at=free[2])
                if ada[1]:
                    load_ada(*ada[1])

            behind = [None, None]

            def ffn_stream(n):
                first = 3 if n == 1 else 2
                for it in range(first):
                    ffn_loads(n, it)
                if n == 3:
                    load_ada(ADA_LAST)
                    load_ada(ADA_LAST + 1)
                with sp.Fori(0, (NIT - first) // 2) as i:
                    ffn_loads(n, first, i)
                    ffn_loads(n, first + 1, i)
                if n != 1:
                    ffn_loads(n, NIT - 1)
                if n == 3:
                    load_ada(ADA_LAST + 2)
                return ada_behind(n, NIT - 1)

            behind = ffn_stream(0)
            for w in range(16):
                load_unit(UNIT_BASE["hgrn"] + w, cols(hg_w_in[0], HG_COL[w]))
                if w < 2:
                    load_ada(*behind[w])
                if w in HG_ADA:
                    load_ada(ADA_HGRN + HG_ADA.index(w))
            for w in range(4):
                load_unit(UNIT_BASE["hgrn"] + 16 + w, cols(hg_w_out[0], w * 256))
            behind = [None, None]
            behind = ffn_stream(1)
            behind = ffn_stream(2)
            for w in range(6):
                load_unit(UNIT_BASE["swa"] + w, cols(sw_w_qkv[0], SW_COL[w]))
                if w == 0:
                    load_ada(*behind[0])
                if w in (1, 2, 5):
                    load_ada(ADA_SWA + w // 2)
            for w in range(4):
                load_unit(UNIT_BASE["swa"] + 6 + w, cols(sw_w_out[0], w * 256))
                if w == 0:
                    load_ada(ADA_SWA + 3)
            behind = [None, None]
            ffn_stream(3)
            for t in range(2):
                half = slice(t * D // 2, (t + 1) * D // 2)
                sp.wait_ge(out_copied, KT * (t + 1))
                sp.dma_start(out[0].rearrange("(g p) d -> p g d", p=P)[:, :, half],
                             mix[:, :, :].rearrange("p (g a) t -> p g (a t)", g=TG)[:, :, half]).then_inc(stored, 16)
            sp.wait_ge(stored, 32)

        q_t, k_t, f_t = m512[0:2], m512[2:4], m512[4:6]
        r_t, kl_t = m512[6], [m512[7], m512[8], m512[16]]
        v_t = m512[9:11]
        at_t = [at_0, ffn_f]
        sg_t = m512[11:13]
        o_t, osd_t = m512[13], m512[14]
        ql_t = [m512[15][:, 0, :], m512[15][:, 1, :], rstd[:, :]]

        rq_t, rk_t = m512[0:4], m512[4:6]
        vt_t, vmix_t = m512[6], m512[7]
        raw_t = m512[8:10]
        rope_t = m512[10:12]
        p_t, pt_t = m512[12:14], m512[14:16]
        rkmix_t = at_0
        Q_BANK = [3, 0, 2, 3]

        def raw_half(slot, half, kind):
            if kind == "D":
                return raw[:, slot, half * HALF:(half + 1) * HALF]
            return raw_cols(slot)[:, :, half * P:(half + 1) * P]

        def ring_half(ring, slot, kind):
            v = ring[:, slot, :]
            return v if kind == "D" else v.rearrange("p (k c) -> p k c", k=KT)

        def split_hi(act, job, unit, half, kind, i=0):
            slot, turn = even(unit, i)
            act.wait_ge(raw_landed[slot], 16 * (turn + 1))
            if job >= JOBS:
                act.wait_ge(w_used, job + 12 * i - JOBS + 1)
            nc.scalar.activation(ring_half(w_hi, job % JOBS, kind), raw_half(slot, half, kind), ACT.Copy)\
                .then_inc(w_hi_ready, 1)

        def split_lo(dve, job, unit, half, kind, i=0):
            slot = unit % RAW
            dve.wait_ge(w_hi_ready, job + 12 * i + 1)
            ins = nc.vector.tensor_tensor(ring_half(w_lo, job % JOBS, kind), raw_half(slot, half, kind),
                                          ring_half(w_hi, job % JOBS, kind).bitcast(F32), ALU.subtract)
            ins.then_inc(w_lo_ready, 1)

        def stage_jobs(b, place):
            if b == 6:
                return []
            name = POST[b]
            u = UNIT_BASE[name]
            if name.startswith("ffn"):
                jobs = [(2 * u, u, 0, "C"), (2 * u + 1, u + 1, 0, "C")] + half_jobs(int(name[3]), 0, 0)
            else:
                jobs = unit_jobs(u) + unit_jobs(u + 1)
            places = {0: {7: jobs[:2], "end": jobs[2:]},
                      2: {1: jobs[:1], 3: jobs[1:3], 5: jobs[3:]},
                      5: {1: jobs[:1], 3: jobs[1:3], 5: jobs[3:]}}.get(b, {"early": jobs[:2], "sums": jobs[2:3], 7: jobs[3:4], "end": jobs[4:]})
            return places.get(place, [])

        def shift_col(b):
            return (b // 3) * 72 + 24 * (b % 3)

        BEHIND = (1, 3, 4, 6)

        def unit_jobs(u):
            return [(2 * u, u, 0, "C"), (2 * u + 1, u, 1, "C")]

        def half_jobs(n, it, hf_):
            u = UNIT_BASE[f"ffn{n}"]
            jb = 2 * u
            if hf_ == 0:
                return [(jb + ffn_job(it, "G1"), u + 3 * it, 1, "C"), (jb + ffn_job(it, "U1"), u + 3 * it + 1, 1, "C"),
                        (jb + ffn_job(it, "D0"), u + 3 * it + 2, 0, "D")]
            jobs = []
            if it < NIT - 1:
                jobs = [(jb + ffn_job(it + 1, "G0"), u + 3 * it + 3, 0, "C"),
                        (jb + ffn_job(it + 1, "U0"), u + 3 * it + 4, 0, "C")]
            return jobs + [(jb + ffn_job(it, "D1"), u + 3 * it + 2, 1, "D")]

        def ffn_splits(n, it, hf_):
            if (it, hf_) == (0, 0):
                return []
            jobs = half_jobs(n, it, hf_)
            return jobs + stage_jobs(BEHIND[n], "early") if (it, hf_) == (NIT - 1, 1) else jobs

        def ada_of(n, it, hf_):
            if n == 3:
                at = 2 * (it - NIT + 2) + hf_
                return (ADA_LAST + at if 0 <= at < 3 else None), 0
            ada0, per = ADA_FFN[n]
            if per == 2:
                return ada0 + 2 * it + hf_, 4
            if per == 1 and hf_ == 0:
                return ada0 + it, 2
            return None, 0

        def ada_before(n, it, hf_):
            if (it, hf_) == (0, 0):
                return None, 0
            return ada_of(n, *((it, 0) if hf_ else (it - 1, 1)))

        def chain_bank(c_):
            return psum[(4, 5, 7)[c_ % 3]][:, :].rearrange("p (a t) -> p a t", a=2)

        RING45 = [("C", 0), ("R", 0), ("C", 1), ("R", 1), ("R", 2), ("R", 3), ("S", 0), ("S", 1), ("R", 4), ("S", 2),
                  ("R", 5)] + [("S", i) for i in range(3, 8)]
        RING_AT = {k: i for i, k in enumerate(RING45)}

        def s_bank(b):
            return 4 + RING_AT[("S", b)] % 2

        def r_bank(r):
            return 4 + RING_AT[("R", r)] % 2

        def p_block(b):
            return p_t[b % 2][:, :, :].rearrange("p a (b t) -> p (a b) t", b=2)

        def pt_block(b):
            return pt_t[b % 2][:, :, :].rearrange("p a (b t) -> p (a b) t", b=2)

        def h_count(b):
            return 8 * b

        def at_view(p):
            return at_t[p % 2][:, :, :].rearrange("p q (b t) -> p q b t", b=2)

        def ql_view(s):
            return ql_t[s % 3].rearrange("p (a t) -> p a t", a=2)

        @block.scalar
        def _(act):
            link = [0]

            def linked(ins):
                link[0] += 1
                ins.then_inc(act_link, 1)
                act.wait_ge(act_link, link[0])

            act.wait_ge(vec_ready, 3)
            nc.scalar.activation(c_act[:, :], vec[:, C_C:C_C + KT], ACT.Silu).then_inc(c_ready, 1)
            act.wait_ge(const_set, 6)
            nc.scalar.activation(small[:, 0:3, :], small[:, 0:3, :], ACT.Exp).then_inc(c_ready, 1)
            act.wait_ge(angle, 1)
            nc.scalar.activation(cosb[:, :], xr[:, 0, :], ACT.Sin).then_inc(c_ready, 1)
            nc.scalar.activation(sinb[:, :], xr[:, 1, :], ACT.Sin).then_inc(c_ready, 1)

            def ada_rows():
                for a in range(ADA_PE):
                    act.wait_ge(ada_pe, a + 1)
                    nc.scalar.activation(ada_row[:, a, :], psum[ROW_BANK[a]][0:1, 0:T], ACT.Copy).then_inc(ada_row_read, 1)

            def stage_part(b):
                for j in stage_jobs(b, "sums"):
                    split_hi(act, *j)
                nc.scalar.activation(warm[:, :], eps_t[:, :], ACT.Sqrt)
                for m in range(KT):
                    act.wait_ge(x_ready, 8 * b + m + 1)
                    if b and m == 0:
                        act.wait_ge(ss_done, 8 * b)
                    nc.scalar.activation(square(m), xT[:, m, :], ACT.Square).then_inc(sq_ready, 1)
                    for j in stage_jobs(b, m) if b or m < KT - 1 else []:
                        split_hi(act, *j)
                act.wait_ge(ss_done, 8 * b + 8)
                nc.scalar.activation(sd[:, :], psum[SUMS][:, 0:T], ACT.Sqrt, bias=eps_t[:, 0:1])\
                    .then_inc(sd_ready, 1)
                if b == 0:
                    ada_rows()
                    for j in stage_jobs(b, KT - 1):
                        split_hi(act, *j)
                act.wait_ge(cols_ready, b + 1)
                for m in range(KT):
                    act.wait_ge(xr_ready, 8 * b + m + 1)
                    g = 8 * b + m
                    if b < 6:
                        sh = shift_col(b) + m
                        nc.scalar.activation(h_hi[:, m, :], xr[:, m % 4, :], ACT.Identity, bias=adac[:, sh:sh + 1])\
                            .then_inc(hf_ready, 1)
                    else:
                        if m >= 4:
                            act.wait_ge(out_t, 2 * (m - 3))
                        nc.scalar.activation(hf[:, m % 4, :], xr[:, m % 4, :], ACT.Copy).then_inc(hf_ready, 1)
                        if m:
                            out_evac(m - 1)
                for j in stage_jobs(b, "end"):
                    split_hi(act, *j)
                if b == 6:
                    out_evac(KT - 1)

            def out_evac(m):
                act.wait_ge(out_t, 2 * m + 2)
                dst = mix[:, :, :].rearrange("p (g a) t -> p g (a t)", g=TG)[:, :, m * P:(m + 1) * P]
                nc.scalar.activation(dst, psum[m % 4][:, 0:T].rearrange("p (g t) -> p g t", g=TG), ACT.Copy)\
                    .then_inc(out_copied, 2)

            def ffn_half(n, it, hf_, i=0):
                for j in ffn_splits(n, it, hf_):
                    split_hi(act, *j, i=i)
                g = NF * n + 2 * it + hf_
                act.wait_ge(w_used, gu_count(n, it, hf_) + 12 * i)
                nc.scalar.activation(sil[:, hf_, :], psum[4 + hf_][:, 0:T], ACT.Silu).then_inc(silu_done, 1)
                act.wait_ge(a_mul, g + 4 * i + 1)
                if it:
                    act.wait_ge(w_used, down_count(n, it - 1, hf_) + 12 * i)
                nc.scalar.activation(a_hi[:, hf_, :], act_f[:, hf_, :], ACT.Copy).then_inc(a_hi_ready, 1)

            def ffn(n):
                for hf_ in range(2):
                    ffn_half(n, 0, hf_)
                with act.Fori(0, (NIT - 3) // 2) as i:
                    for it in (1, 2):
                        for hf_ in range(2):
                            ffn_half(n, it, hf_, i)
                for it in (NIT - 2, NIT - 1):
                    for hf_ in range(2):
                        ffn_half(n, it, hf_)

            def hgrn():
                u = UNIT_BASE["hgrn"]
                evac = [0]
                act.wait_ge(lb_ready, 1)

                def proj_evac(w):
                    bank = psum[w % 4][:, :].rearrange("p (a t) -> p a t", a=2)
                    act.wait_ge(w_used, 2 * (u + w + 1))
                    if w < 12 and w % 3 == 2:
                        p = w // 3
                        if p >= 2:
                            act.wait_ge(chain_mm, STEP_AT[(p - 2, "O")] + 1)
                        nc.scalar.activation(v_t[p % 2][:, :, :], bank, ACT.Copy).then_inc(proj_read, 1)
                        return
                    if evac[0]:
                        act.wait_ge(gates_used, evac[0])
                    if w >= 12 or w % 3 == 0:
                        evac[0] += 1
                        if w:
                            act.wait_ge(fk_ready, min(w // 3, NP_HG))
                    ins = nc.scalar.activation(sg_t[0][:, :, :], bank, ACT.Sigmoid)
                    if w < 12 and w % 3 == 0:
                        ins = nc.scalar.activation(sg_t[1][:, :, :], bank, ACT.Copy)
                    elif w < 12:
                        ins = nc.scalar.activation(sg_t[1][:, :, :], bank, ACT.Sigmoid, scale=-1.0)
                    ins.then_inc(proj_read, 1)
                    if w < 12 and w % 3 == 1:
                        p = w // 3
                        act.wait_ge(proj_read, w + 1)
                        if p >= 2:
                            act.wait_ge(chain_mm, STEP_AT[(p - 2, 7)] + 1)
                        for hh in range(2):
                            j = 2 * p + hh
                            nc.scalar.activation(f_t[p % 2][:, hh, :], sg_t[0][:, hh, :], ACT.Identity,
                                                 scale=oml[:, j:j + 1], bias=lb[:, j:j + 1])
                            ins = nc.scalar.activation(k_t[p % 2][:, hh, :], sg_t[1][:, hh, :], ACT.Copy,
                                                       scale=oml[:, j:j + 1])
                        ins.then_inc(fk_ready, 1)

                def mix_round(p):
                    act.wait_ge(gates_used, NP_HG + p + 1)
                    nc.scalar.activation(h_hi[:, 2 * p:2 * p + 2, :], mix[:, 2 * p:2 * p + 2, :], ACT.Copy)\
                        .then_inc(mix_hi, 1)

                for w in range(18):
                    if w == 16:
                        act.wait_ge(w_used, 2 * (u + 16))
                        for p in range(NP_HG - 1):
                            mix_round(p)
                    if 1 <= w <= 16:
                        proj_evac(w - 1)
                    if w < 16:
                        for j in unit_jobs(u + w + 2):
                            split_hi(act, *j)
                    for c_, (ws, p, s) in enumerate(STEPS):
                        if ws != w:
                            continue
                        if s == "O":
                            act.wait_ge(chain_mm, c_ + 1)
                            if p:
                                act.wait_ge(o_normed, p)
                            nc.scalar.activation(o_t[:, :, :], chain_bank(c_), ACT.Copy)
                            nc.scalar.activation(osd_t[:, :, :], chain_bank(c_), ACT.Square)\
                                .then_inc(osq_ready, 1)
                        if s == "S":
                            act.wait_ge(chain_mm, c_ + 1)
                            nc.scalar.activation(osd[:, :], chain_bank(c_)[:, 0, 0:2 * TG], ACT.Sqrt, scale=8.0,
                                                 bias=eps_t[:, 0:1]).then_inc(osd_ready, 1)
                mix_round(NP_HG - 1)
                for w in range(18, 20):
                    for j in unit_jobs(u + w):
                        split_hi(act, *j)

            def swa():
                u = UNIT_BASE["swa"]

                def evac(w):
                    if w == 1:
                        return
                    act.wait_ge(w_used, 2 * (u + w + 1))
                    i = w - 1 if w else 0
                    bank = psum[0 if w == 0 else Q_BANK[i - 1]]
                    col = C_BQ + (2 * (i - 1) if w else KT)
                    if i >= 2:
                        act.wait_ge(rope_done, i)
                    for t in range(2):
                        nc.scalar.activation(raw_t[i % 2][:, t, :], bank[:, t * T:(t + 1) * T], ACT.Identity,
                                             bias=vec[:, col + t:col + t + 1]).then_inc(sw_evac, 1)

                def softmax(b):
                    n = b % 4
                    keys = CH if n == 0 else 2 * CH
                    act.wait_ge(s_max, b + 1)
                    if b >= 2:
                        act.wait_ge(pt_mm, b - 1)
                    for j in range(4):
                        nc.scalar.activation(p_block(b)[:, j, 0:keys], psum[s_bank(b)][:, j * P:j * P + keys],
                                             ACT.Exp, scale=0.125, bias=stat[:, b % 2, 2, j:j + 1],
                                             accum_out=stat[:, b % 2, 4, j:j + 1]).then_inc(p_exp, 1)
                    nc.scalar.activation(stat[:, b % 2, 5, :], stat[:, b % 2, 3, :], ACT.Exp).then_inc(p_exp, 1)

                def pt_copy(b):
                    keys = CH if b % 4 == 0 else 2 * CH
                    act.wait_ge(pt_mm, b + 1)
                    if b >= 2:
                        act.wait_ge(o_mm, b - 1)
                    nc.scalar.activation(pt_t[b % 2][0:keys, :, :],
                                         psum[6 + b % 2][0:keys, :].rearrange("p (a t) -> p a t", a=2), ACT.Copy)\
                        .then_inc(pt_copied, 1)

                def k_mix(r):
                    act.wait_ge(rope_done, r + 1)
                    for t, chunk in enumerate((2, 1)):
                        ins = nc.scalar.activation(rkmix_t[:, 2 * r:2 * r + 2, t * CH:(t + 1) * CH],
                                                   rk_t[r][:, :, chunk * CH:(chunk + 1) * CH], ACT.Copy)
                    ins.then_inc(k_mixed, 1)

                def split_unit(w):
                    for j in unit_jobs(u + w):
                        split_hi(act, *j)

                for w in range(4):
                    split_unit(w + 2)
                    if w:
                        evac(w - 1)
                    if w == 3:
                        k_mix(0)
                        k_mix(1)
                evac(3)
                split_unit(6)
                evac(4)
                split_unit(7)
                softmax(0)
                softmax(1)
                evac(5)
                pt_copy(0)
                for b in range(2, 8):
                    softmax(b)
                    pt_copy(b - 1)
                    if b == 5:
                        for jp in range(2):
                            o_split(jp)
                pt_copy(7)
                for jp in range(2, 4):
                    o_split(jp)
                split_unit(8)
                split_unit(9)

            def o_split(jp):
                act.wait_ge(o_mm, 4 * (jp // 2) + 4)
                nc.scalar.activation(h_hi[:, 2 * jp:2 * jp + 2, :], psum[jp][:, :].rearrange("p (a t) -> p a t", a=2),
                                     ACT.Copy).then_inc(mix_hi, 1)

            stage_part(0)
            ffn(0)
            stage_part(1)
            hgrn()
            stage_part(2)
            ffn(1)
            stage_part(3)
            ffn(2)
            stage_part(4)
            swa()
            stage_part(5)
            ffn(3)
            stage_part(6)

        @block.gpsimd
        def _(pool):
            for b in range(7):
                for m in (0, 2, 4):
                    pool.wait_ge(sq_ready, 8 * b + m + 2)
                    nc.gpsimd.tensor_tensor(square(m), square(m), square(m + 1), ALU.add).then_inc(sq_pair, 1)

        @block.tensor
        def _(pe):
            def product(dst, hi, lo, rhi, rlo, first, last, group=False):
                nc.tensor.matmul(dst, hi, rhi, start=first, stop=False, skip_group_check=group)
                nc.tensor.matmul(dst, hi, rlo, start=False, stop=False, skip_group_check=group)
                return nc.tensor.matmul(dst, lo, rhi, start=False, stop=last, skip_group_check=group)

            def w_tiles(job, k):
                s = job % JOBS
                return w_hi[:, s, k * P:(k + 1) * P], w_lo[:, s, k * P:(k + 1) * P]

            pe.wait_ge(const_in, 32)
            pe.wait_ge(small_in, 16 * 9)
            for t, n in ((0, 72), (1, 72), (2, C_ROWS)):
                nc.tensor.transpose(psum[4][:, t * P:t * P + n], stage[0:n, t, :], con[0:n, K_ID:K_ID + n])\
                    .then_inc(stage_t, 1)
            pe.wait_ge(x_in, 16 * 4)
            xin = mix[:, :, :].rearrange("p (g a) t -> p g (a t)", g=TG)
            for m in range(KT):
                for g in range(TG):
                    ins = nc.tensor.transpose(y_acc(m)[:, g * P:(g + 1) * P], xin[:, g, m * P:(m + 1) * P],
                                              con[:, K_ID:K_ID + P])
                ins.then_inc(y_done, 1)
            pe.wait_ge(const_set, 6)

            def ada_reduce(a, step=0, i=0):
                pe.wait_ge(ada_step, 8 * made(a) + 8 * step * i + 8)
                if made(a):
                    pe.wait_ge(ada_out, made(a) + step * i)
                col = 2 * (a % 2)
                for t in range(2):
                    ins = nc.tensor.matmul(psum[ADA_BANK][:, col + t:col + t + 1],
                                           acc[:, a % 2, t * P:(t + 1) * P], ones[:, 0:1], start=True, stop=True)
                ins.then_inc(ada_sum, 1)

            def ada_product(a):
                place, landed = ada_place(a)
                w = place.rearrange("p (k c) -> p k c", k=KT)
                pe.wait_ge(landed, 16)
                if a == 0:
                    pe.wait_ge(vec_ready, 3)
                else:
                    pe.wait_ge(x_ready, 2 * a + 2)
                for k in range(KT):
                    ins = nc.tensor.matmul(psum[ROW_BANK[a]][0:1, 0:T], c_act[:, k:k + 1], w[:, k, :], start=(k == 0),
                                           stop=(k == KT - 1))
                ins.then_inc(ada_pe, 1)

            def ada_turn_row(a):
                pe.wait_ge(ada_row_read, a + 1)
                for t in range(2):
                    ins = nc.tensor.matmul(psum[5][:, 2 * a + t:2 * a + t + 1], ada_row[:, a, t * P:(t + 1) * P],
                                           ones[0:1, 0:1], start=True, stop=True)
                ins.then_inc(ada_turned, 1)

            def mean_squares(b):
                for m in (0, 2, 4, 6, 7):
                    if m < 6:
                        pe.wait_ge(sq_pair, 3 * b + m // 2 + 1)
                    else:
                        pe.wait_ge(sq_ready, 8 * b + m + 1)
                    if b and m == 0:
                        pe.wait_ge(sd_ready, b)
                    nc.tensor.matmul(psum[SUMS][:, 0:T], inv_d[:, :], square(m), start=(m == 0),
                                     stop=(m == KT - 1)).then_inc(ss_done, 2 if m < 6 else 1)

            pe.wait_ge(c_ready, 1)
            ada_product(0)
            ada_product(1)
            mean_squares(0)
            for a in range(ADA_PE):
                ada_turn_row(a)
                ada_reduce(ADA_PE + a)
                if a + 2 < ADA_PE:
                    ada_product(a + 2)

            def gate_up(n, it, hf_, i=0):
                u = UNIT_BASE[f"ffn{n}"]
                jg = 2 * u + ffn_job(it, f"G{hf_}")
                b = (0, 2, 3, 5)[n]
                g = NF * n + 2 * it + hf_
                pe.wait_ge(w_lo_ready, jg + 12 * i + 2)
                if g >= 2:
                    pe.wait_ge(a_mul, g + 4 * i - 1)
                for k in range(KT):
                    if it == 0 and hf_ == 0:
                        pe.wait_ge(h_lo_ready, h_count(b) + k + 1)
                    for t in range(2):
                        hi, lo = w_tiles(jg + t, k)
                        ins = product(psum[4 + hf_][:, t * T:(t + 1) * T], hi, lo, h_hi[:, k, :], h_lo[:, k, :],
                                      k == 0 and t == 0, k == KT - 1, group=True)
                ins.then_inc(w_used, 2)

            def down(n, it, hf_, i=0, first=False, last=False):
                u = UNIT_BASE[f"ffn{n}"]
                job = 2 * u + ffn_job(it, f"D{hf_}")
                g = NF * n + 2 * it + hf_
                pe.wait_ge(w_lo_ready, job + 12 * i + 1)
                pe.wait_ge(a_lo_ready, g + 4 * i + 1)
                for m in range(KT):
                    hi, lo = w_tiles(job, m)
                    ins = product(y_acc(m), hi, lo, a_hi[:, hf_, :], a_lo[:, hf_, :], first and m % 2 == 0, last,
                                  group=True)
                    if last:
                        ins.then_inc(y_done, 1)
                if last:
                    pe.wait_ge(y_done, 8 * Y_STAGES.index((1, 3, 4, 6)[n]) + 8)
                    pe.sem_inc(w_used, 1)
                else:
                    ins.then_inc(w_used, 1)

            def iteration(n, it, i=0):
                for hf_ in range(2):
                    gate_up(n, it, hf_, i)
                    a, step = ada_before(n, it, hf_)
                    if a is not None:
                        ada_reduce(a, step, i)
                    if hf_ == 1:
                        down(n, it, 0, i, first=(it == 0))
                    elif it:
                        down(n, it - 1, 1, i)

            def ffn(n):
                iteration(n, 0)
                with pe.Fori(0, (NIT - 3) // 2) as i:
                    for it in (1, 2):
                        iteration(n, it, i)
                iteration(n, NIT - 2)
                iteration(n, NIT - 1)
                down(n, NIT - 1, 1, last=True)
                last = ada_of(n, NIT - 1, 1)[0]
                if last is not None:
                    ada_reduce(last)

            def proj(unit, bank, b, first, tiles=(0, 1)):
                if first:
                    pe.wait_ge(w_lo_ready, 2 * unit + 2)
                    for k in range(KT):
                        pe.wait_ge(h_lo_ready, h_count(b) + k + 1)
                        for t in range(2):
                            hi, lo = w_tiles(2 * unit + t, k)
                            ins = product(bank[:, t * T:(t + 1) * T], hi, lo, h_hi[:, k, :], h_lo[:, k, :],
                                          k == 0 and t == 0, k == KT - 1, group=True)
                    ins.then_inc(w_used, 2)
                    return
                for t in tiles:
                    pe.wait_ge(w_lo_ready, 2 * unit + t + 1)
                    for k in range(KT):
                        hi, lo = w_tiles(2 * unit + t, k)
                        ins = product(bank[:, t * T:(t + 1) * T], hi, lo, h_hi[:, k, :], h_lo[:, k, :],
                                      k == 0, k == KT - 1)
                    ins.then_inc(w_used, 1)

            def proj_tokens(unit, bank):
                pe.wait_ge(w_lo_ready, 2 * unit + 2)
                s = (2 * unit) % JOBS
                for g in range(TG):
                    tok = slice(g * P, (g + 1) * P)
                    for k in range(KT):
                        wh = w_hi[:, s:s + 2, k * P:(k + 1) * P]
                        wl = w_lo[:, s:s + 2, k * P:(k + 1) * P]
                        ins = product(bank[:, g * T:(g + 1) * T], h_hi[:, k, tok], h_lo[:, k, tok], wh, wl,
                                      k == 0, k == KT - 1)
                ins.then_inc(w_used, 2)

            def out_part(u, b, m, ks):
                unit, t = u + m // 2, m % 2
                if 0 in ks:
                    pe.wait_ge(w_lo_ready, 2 * unit + t + 1)
                for k in ks:
                    if m == 0 or k == ks[0]:
                        pe.wait_ge(mix_lo, 4 * (b == 5) + k // 2 + 1)
                    hi, lo = w_tiles(2 * unit + t, k)
                    ins = product(y_acc(m), hi, lo, h_hi[:, k, :], h_lo[:, k, :], k == 0 and t == 0, k == KT - 1,
                                  group=True)
                if KT - 1 in ks:
                    ins.then_inc(w_used, 1)

            def hgrn():
                u = UNIT_BASE["hgrn"]

                def chain(c_, p, s):
                    if c_ >= 3:
                        _, pp, prev = STEPS[c_ - 3]
                        if prev == "O":
                            pe.wait_ge(osq_ready, pp + 1)
                        elif prev == "S":
                            pe.wait_ge(osd_ready, pp + 1)
                        elif prev == "B":
                            pe.wait_ge(o_normed, pp + 1)
                        else:
                            pe.wait_ge(chain_read_dve, sum(x_[2] not in ("O", "S", "B") for x_ in STEPS[:c_ - 2]))
                    bank = chain_bank(c_)
                    q, k = q_t[p % 2], k_t[p % 2]
                    if s == "D":
                        pe.wait_ge(gates_used, p + 1)
                        pe.wait_ge(fk_ready, p + 1)
                        for hh in range(2):
                            for g in range(TG):
                                tok = slice(g * P, (g + 1) * P)
                                ins = nc.tensor.matmul(bank[:, hh, tok], k[:, hh, tok], q[:, hh, tok],
                                                       start=True, stop=True)
                    elif s == "O":
                        pe.wait_ge(chain_read_dve, 9 * (p + 1))
                        pe.wait_ge(proj_read, 3 * p + 3)
                        v, at = v_t[p % 2], at_view(p)
                        for hh in range(2):
                            vc = slice(hh * P, (hh + 1) * P)
                            nc.tensor.matmul(bank[:, hh, :], v[:, 0, vc], at_t[p % 2][:, 2 * hh, :],
                                             start=True, stop=False, skip_group_check=True)
                            ins = nc.tensor.matmul(bank[:, hh, P:T], v[:, 1, vc], at[:, 2 * hh + 1, 0, :],
                                                   start=False, stop=True, skip_group_check=True)
                    elif s == "S":
                        pe.wait_ge(osq_ready, p + 1)
                        for g in range(2 * TG):
                            ins = nc.tensor.matmul(bank[:, 0, g:g + 1], osd_t[:, g // TG, (g % TG) * P:(g % TG + 1) * P],
                                                   inv_d[:, 0:1], start=True, stop=True)
                    elif s == "B":
                        pe.wait_ge(orstd_ready, p + 1)
                        for g in range(2 * TG):
                            ins = nc.tensor.matmul(bank[:, g // TG, (g % TG) * P:(g % TG + 1) * P],
                                                   orstd[:, g:g + 1].broadcast_to([P, P]), con[:, K_ID:K_ID + P],
                                                   start=True, stop=True)
                    else:
                        pe.wait_ge(chain_in, 8 * p + s + 1)
                        kl = k if s == 0 else kl_t[s % 3]
                        ql = ql_view(s)
                        for hh in range(2):
                            if s == 7:
                                ins = nc.tensor.matmul(bank[:, 0, hh * P:(hh + 1) * P], kl[:, hh, 0:P],
                                                       ql[:, hh, :], start=True, stop=True)
                                continue
                            for g in range(TG):
                                ins = nc.tensor.matmul(bank[:, 0, (hh * TG + g) * 64:(hh * TG + g + 1) * 64],
                                                       kl[:, hh, g * P:(g + 1) * P], ql[:, hh, g * 64:(g + 1) * 64],
                                                       start=True, stop=True)
                    ins.then_inc(chain_mm, 1)

                late = []

                def late_step():
                    if late:
                        chain(*late.pop())

                for w in range(18):
                    if w < 16:
                        if w >= 4:
                            pe.wait_ge(proj_read, w - 3)
                        if w == 0:
                            proj(u, psum[0], 1, True)
                        elif w < 12 and w % 3 == 2:
                            late_step()
                            proj_tokens(u + w, psum[w % 4])
                        else:
                            proj(u + w, psum[w % 4], 1, False, (0,))
                            late_step()
                            proj(u + w, psum[w % 4], 1, False, (1,))
                    for c_, (ws, p, s) in enumerate(STEPS):
                        if ws == w:
                            if s in (1, 4, 7):
                                late.append((c_, p, s))
                            else:
                                chain(c_, p, s)
                    if w >= 16:
                        pe.wait_ge(proj_read, w - 3)
                        for m in (2 * w - 32, 2 * w - 31):
                            out_part(u + 16, 2, m, range(2 * NP_HG - 2))
                    if w - 1 in HG_ADA:
                        ada_reduce(ADA_HGRN + HG_ADA.index(w - 1))
                for m in range(4):
                    out_part(u + 16, 2, m, range(2 * NP_HG - 2, KT))
                pe.wait_ge(proj_read, 16)
                for m in range(4, KT):
                    out_part(u + 16, 2, m, range(KT))

            def swa():
                u = UNIT_BASE["swa"]

                def ring_wait(i):
                    if i < 2:
                        return
                    kind, j = RING45[i - 2]
                    if kind in "CR":
                        pe.wait_ge(rope_done, j + 1)
                    else:
                        pe.wait_ge(p_exp, 5 * (j + 1))

                def rotate(r):
                    pe.wait_ge(sw_evac, 2 * max(r, 1))
                    for what in ("C", "R") if r < 2 else ("R",):
                        ring_wait(RING_AT[(what, r)])
                        bank = psum[4 + RING_AT[(what, r)] % 2]
                        if r < 2:
                            for t in range(2):
                                c0 = K_DUP + (t if what == "C" else 2 + t) * P
                                ins = nc.tensor.matmul(bank[:, t * T:(t + 1) * T], con[:, c0:c0 + P],
                                                       raw_t[0][:, r, :], start=True, stop=True)
                        else:
                            ins = nc.tensor.matmul(bank[:, :].rearrange("p (a t) -> p a t", a=2),
                                                   con[:, K_PERM:K_PERM + P], raw_t[(r - 1) % 2][:, :, :],
                                                   start=True, stop=True)
                    ins.then_inc(rope_mm, 1)

                def scores(b):
                    jh, n = b // 4, b % 4
                    ring_wait(RING_AT[("S", b)])
                    pe.wait_ge(rope_done, 4 + 2 * jh)
                    if n == 2:
                        pe.wait_ge(k_mixed, jh + 1)
                    keys = {0: slice(0, CH), 1: slice(0, 2 * CH), 2: slice(0, 2 * CH), 3: slice(2 * CH, 4 * CH)}[n]
                    for hh in range(2):
                        if hh:
                            pe.wait_ge(s_half, b + 1)
                        for rr in range(2):
                            half = slice(64 * hh, 64 * hh + 64)
                            k = rkmix_t[half, 2 * jh + rr, keys] if n == 2 else rk_t[jh][half, rr, keys]
                            q = rq_t[2 * jh + rr][half, :, :].rearrange("p a t -> p (a t)")[:, n * P:(n + 1) * P]
                            col = (2 * rr + hh) * P
                            ins = nc.tensor.matmul(psum[s_bank(b)][:, col:col + keys.stop - keys.start], q, k,
                                                   start=True, stop=True)
                        if hh == 0:
                            ins.then_inc(s_half, 1)
                    ins.then_inc(s_mm, 1)

                def turn(b):
                    keys = CH if b % 4 == 0 else 2 * CH
                    pe.wait_ge(p_norm, b + 1)
                    if b >= 2:
                        pe.wait_ge(pt_copied, b - 1)
                    elif b == 0:
                        pe.wait_ge(ada_out, made(ADA_LAST))
                    for jj in range(4):
                        ins = nc.tensor.transpose(psum[6 + b % 2][0:keys, jj * P:(jj + 1) * P],
                                                  p_block(b)[:, jj, 0:keys], con[:, K_ID:K_ID + P])
                    ins.then_inc(pt_mm, 1)

                def outputs(b):
                    jh, n = b // 4, b % 4
                    keys = CH if n == 0 else 2 * CH
                    pe.wait_ge(pt_copied, b + 1)
                    pe.wait_ge(sw_v, 2)
                    for rr in range(2):
                        r = 2 * jh + rr
                        if n == 2:
                            v = vmix_t[:, 0, r * 64:(r + 1) * 64]
                        else:
                            v = vt_t[0:keys, n // 2, r * 64:(r + 1) * 64]
                        for hh in range(2):
                            dst = psum[r][64 * hh:64 * hh + 64, :].rearrange("p (a t) -> p a t", a=2)
                            ins = nc.tensor.matmul(dst[:, :, n * CH:(n + 1) * CH], v,
                                                   pt_block(b)[0:keys, 2 * rr + hh, :].rearrange(
                                                       "p (a t) -> p a t", a=2), start=True, stop=True)
                    ins.then_inc(o_mm, 1)

                def q_tile(i, t):
                    proj(u + 2 + i, psum[Q_BANK[i]], 4, False, (t,))

                proj(u, psum[0], 4, True)
                proj_tokens(u + 1, psum[2])
                rotate(0)
                ada_reduce(ADA_SWA)
                q_tile(0, 0)
                rotate(1)
                q_tile(0, 1)
                ada_reduce(ADA_SWA + 1)
                pe.wait_ge(sw_evac, 2)
                q_tile(1, 0)
                rotate(2)
                q_tile(1, 1)
                ada_reduce(ADA_SWA + 2)
                pe.wait_ge(sw_v, 1)
                q_tile(2, 0)
                rotate(3)
                q_tile(2, 1)
                ada_reduce(ADA_SWA + 3)
                pe.wait_ge(sw_evac, 4)
                q_tile(3, 0)
                scores(0)
                q_tile(3, 1)
                scores(1)
                rotate(4)
                turn(0)
                scores(2)
                rotate(5)
                for b in range(2, 9):
                    turn(b - 1)
                    outputs(b - 2)
                    if b < 7:
                        scores(b + 1)
                    if b >= 6:
                        out_part(u + 6, 5, b - 6, range(4))
                out_part(u + 6, 5, 3, range(4))
                outputs(7)
                for m in range(4):
                    out_part(u + 6, 5, m, range(4, KT))
                for m in range(4, KT):
                    out_part(u + 6, 5, m, range(KT))

            ffn(0)
            mean_squares(1)
            hgrn()
            mean_squares(2)
            ffn(1)
            mean_squares(3)
            ffn(2)
            mean_squares(4)
            swa()
            mean_squares(5)
            ffn(3)
            mean_squares(6)
            for m in range(KT):
                pe.wait_ge(hf_ready, 48 + m + 1)
                if m >= 4:
                    pe.wait_ge(out_copied, 2 * (m - 3))
                for g in range(TG):
                    ins = nc.tensor.transpose(psum[m % 4][:, g * P:(g + 1) * P], hf[:, m % 4, g * P:(g + 1) * P],
                                              con[:, K_ID:K_ID + P])
                ins.then_inc(out_t, 2)

        @block.vector
        def _(dve):
            link = [0]

            def step(ins):
                link[0] += 1
                ins.then_inc(dve_link, 1)

            def linked(ins):
                step(ins)
                dve.wait_ge(dve_link, link[0])

            nc.vector.memset(ones[:, :], 1.0).then_inc(const_set, 1)
            nc.vector.memset(inv_d[:, :], 1.0 / D).then_inc(const_set, 1)
            nc.vector.memset(eps_t[:, :], EPS).then_inc(const_set, 1)
            dve.wait_ge(const_in, 32)
            nc.vector.tensor_copy(mask_t[:, :, :].rearrange("p a b -> p (a b)"),
                                  hf[:, 0:2, :].rearrange("p a t -> p (a t)")[:, 0:448])
            for t, (dst, n) in enumerate(((adab[:, 0:72], 72), (adab[:, 72:144], 72), (vec[:, :], C_ROWS))):
                dve.wait_ge(stage_t, 3)
                nc.vector.tensor_copy(dst, psum[4][:, t * P:t * P + n]).then_inc(vec_ready, 1)
            dve.wait_ge(vec_ready, 3)
            lbr = vec[:, C_LB:C_LB + 24].rearrange("p (l a) -> p l a", l=3)
            linked(nc.vector.tensor_tensor(small[:, 3, :], lbr[:, 0, :], lbr[:, 1, :], ALU.max))
            linked(nc.vector.tensor_tensor(small[:, 3, :], small[:, 3, :], lbr[:, 2, :], ALU.max))
            for r in range(3):
                nc.vector.tensor_tensor(small[:, r, :], lbr[:, r, :], small[:, 3, :], ALU.subtract)\
                    .then_inc(const_set, 1)
            dve.wait_ge(const_set, 6)
            dve.wait_ge(x_in, 16 * 4)
            for t in range(2):
                half = slice(64 * t, 64 * t + 64)
                linked(nc.vector.tensor_copy(sink[half, :].rearrange("p (r h) -> p r h", h=2),
                                             sink_all[half, :].rearrange("p (r a h) -> p a r h", a=2, h=2)[:, t]))
            linked(nc.vector.tensor_copy(cosb[:, :], sinb[:, :].bitcast(I32)))
            linked(nc.vector.tensor_scalar(xr[:, 0, :], cosb[:, :], con[:, K_FREQ:K_FREQ + 1], None, ALU.mult))
            linked(nc.vector.tensor_scalar(xr[:, 1, :], xr[:, 0, :], float(0.5 / np.pi), MAGIC, ALU.mult, ALU.add))
            linked(nc.vector.tensor_scalar(xr[:, 1, :], xr[:, 1, :], MAGIC, None, ALU.subtract))
            parts = (6.28125, 0.0019340515136718750, float(2 * np.pi - 6.28125 - 0.0019340515136718750))
            for part in parts:
                linked(nc.vector.scalar_tensor_tensor(out=xr[:, 0, :], in0=xr[:, 1, :], scalar=-part,
                                                      in1=xr[:, 0, :], op0=ALU.mult, op1=ALU.add))
            linked(nc.vector.tensor_scalar(xr[:, 1, :], xr[:, 0, :], 3.1415925, -3.1415925, ALU.min, ALU.max))
            linked(nc.vector.tensor_scalar(xr[:, 0, :], xr[:, 1, :], -1.0, None, ALU.mult))
            linked(nc.vector.tensor_tensor(xr[:, 0, :], xr[:, 0, :], xr[:, 1, :], ALU.min))
            nc.vector.tensor_scalar(xr[:, 0, :], xr[:, 0, :], float(np.pi / 2), None, ALU.add).then_inc(angle, 1)

            def ada_steps(a, step=0, i=0):
                place, landed = ada_place(a)
                w = place.rearrange("p (k c) -> p k c", k=KT)

                def one(k):
                    if k == 0:
                        dve.wait_ge(landed, 16 * ada_turn(a) + 8 * step * i)
                        nc.vector.tensor_scalar(acc[:, a % 2, :], w[:, 0, :], c_act[:, 0:1], None, ALU.mult)\
                            .then_inc(ada_step, 1)
                        return
                    dve.wait_ge(ada_step, 8 * made(a) + 8 * step * i + k)
                    nc.vector.scalar_tensor_tensor(out=acc[:, a % 2, :], in0=w[:, k, :], scalar=c_act[:, k:k + 1],
                                                   in1=acc[:, a % 2, :], op0=ALU.mult, op1=ALU.add).then_inc(ada_step, 1)
                return one

            def ada_finish(a, step=0, i=0):
                dve.wait_ge(ada_sum, made(a) + step * i + 1)
                col = 2 * (a % 2)
                at = bass.ds(2 * a + 2 * step * i, 2)
                nc.vector.tensor_tensor(adac[:, at], psum[ADA_BANK][:, col:col + 2], adab[:, at], ALU.add)\
                    .then_inc(ada_out, 1)

            dve.wait_ge(c_ready, 1)
            for a in range(ADA_PE, ADA_START):
                if a == ADA_PE:
                    for m in range(KT):
                        dve.wait_ge(y_done, (m | 1) + 1)
                        nc.vector.tensor_copy(xT[:, m, :], y_acc(m)).then_inc(x_ready, 1)
                one = ada_steps(a)
                for k in range(KT):
                    one(k)
                if a > ADA_PE:
                    ada_finish(a - 1)
                if a == ADA_START - 3:
                    dve.wait_ge(sd_ready, 1)
                    linked(nc.vector.reciprocal(rstd[:, :], sd[:, :]))
            ada_finish(ADA_START - 1)
            dve.wait_ge(ada_turned, ADA_PE)
            linked(nc.vector.tensor_tensor(adac[:, 0:2 * ADA_PE], psum[5][:, 0:2 * ADA_PE], adab[:, 0:2 * ADA_PE],
                                           ALU.add))

            def stage_part(b):
                for j in stage_jobs(b, "sums"):
                    split_lo(dve, *j)
                dve.wait_ge(ada_out, made(ADA_NEEDED[b]))
                if b:
                    r = b - 1
                    gc = (r // 3) * 72 + 24 * (r % 3) + 16
                    linked(nc.vector.tensor_scalar(gcol[:, :], adac[:, gc:gc + KT], 1.0 if r % 3 == 1 else 0.5,
                                                   None, ALU.mult))
                if b < 6:
                    sc = (b // 3) * 72 + 24 * (b % 3) + 8
                    ng = C_NORM + 8 * b
                    nc.vector.scalar_tensor_tensor(out=scol[:, :], in0=adac[:, sc:sc + KT], scalar=1.0,
                                                   in1=vec[:, ng:ng + KT], op0=ALU.add, op1=ALU.mult)\
                        .then_inc(cols_ready, 1)
                else:
                    nc.vector.tensor_copy(scol[:, :], vec[:, C_FINAL:C_FINAL + KT]).then_inc(cols_ready, 1)
                dve.wait_ge(cols_ready, b + 1)
                if b == 5:
                    linked(nc.vector.tensor_tensor(small[:, 5, :], gcol[:, :], vec[:, C_BO:C_BO + KT], ALU.mult))
                for m in range(KT if b else 0):
                    y_wait(dve, b, m)
                    if b == 5:
                        linked(nc.vector.tensor_scalar(xT[:, m, :], xT[:, m, :], small[:, 5, m:m + 1], None,
                                                       ALU.add))
                    nc.vector.scalar_tensor_tensor(out=xT[:, m, :], in0=y_acc(m), scalar=gcol[:, m:m + 1],
                                                   in1=xT[:, m, :], op0=ALU.mult, op1=ALU.add).then_inc(x_ready, 1)
                    for j in stage_jobs(b, m):
                        split_lo(dve, *j)
                dve.wait_ge(x_ready, 8 * b + 8)
                if b == 0:
                    for j in stage_jobs(b, KT - 1):
                        split_lo(dve, *j)
                if b in BEHIND[:3]:
                    last = ada_of(BEHIND.index(b), NIT - 1, 1)[0]
                    if last is not None:
                        ada_finish(last)
                if b:
                    dve.wait_ge(sd_ready, b + 1)
                    linked(nc.vector.reciprocal(rstd[:, :], sd[:, :]))
                for m in range(KT + 1):
                    g = 8 * b + m
                    if m < KT:
                        if m >= 4:
                            dve.wait_ge(hf_ready, g - 3)
                        nc.vector.scalar_tensor_tensor(out=xr[:, m % 4, :], in0=xT[:, m, :],
                                                       scalar=scol[:, m:m + 1], in1=rstd[:, :], op0=ALU.mult,
                                                       op1=ALU.mult).then_inc(xr_ready, 1)
                    if m and b < 6:
                        dve.wait_ge(hf_ready, g)
                        sh = shift_col(b) + m - 1
                        nc.vector.scalar_tensor_tensor(out=h_lo[:, m - 1, :], in0=xr[:, (m - 1) % 4, :],
                                                       scalar=adac[:, sh:sh + 1],
                                                       in1=h_hi[:, m - 1, :].bitcast(F32), op0=ALU.add,
                                                       op1=ALU.subtract).then_inc(h_lo_ready, 1)
                for j in stage_jobs(b, "end"):
                    split_lo(dve, *j)

            def ffn_half(n, it, hf_, i=0):
                jobs = ffn_splits(n, it, hf_)
                a, step = ada_of(n, it, hf_)
                one = ada_steps(a, step, i) if a is not None else None

                def ada(k):
                    if one:
                        one(k)

                for t in range(3):
                    if t < len(jobs):
                        split_lo(dve, *jobs[t], i=i)
                    ada(t)
                for j in jobs[3:]:
                    split_lo(dve, *j, i=i)
                ada(3)
                ada(4)
                g = NF * n + 2 * it + hf_
                dve.wait_ge(silu_done, g + 4 * i + 1)
                nc.vector.tensor_tensor(act_f[:, hf_, :], sil[:, hf_, :], psum[4 + hf_][:, T:2 * T], ALU.mult)\
                    .then_inc(a_mul, 1)
                ada(5)
                dve.wait_ge(a_hi_ready, g + 4 * i + 1)
                nc.vector.tensor_tensor(a_lo[:, hf_, :], act_f[:, hf_, :], a_hi[:, hf_, :].bitcast(F32),
                                        ALU.subtract).then_inc(a_lo_ready, 1)
                ada(6)
                ada(7)
                prev, prev_step = ada_before(n, it, hf_)
                if prev is not None:
                    ada_finish(prev, prev_step, i)

            def ffn(n):
                for hf_ in range(2):
                    ffn_half(n, 0, hf_)
                with dve.Fori(0, (NIT - 3) // 2) as i:
                    for it in (1, 2):
                        for hf_ in range(2):
                            ffn_half(n, it, hf_, i)
                for it in (NIT - 2, NIT - 1):
                    for hf_ in range(2):
                        ffn_half(n, it, hf_)

            def halves(ap, h):
                v = ap.rearrange("p a (n b h) -> p a n b h", b=2, h=h)
                return v[:, :, :, 0, :], v[:, :, :, 1, :]

            def hgrn():
                u = UNIT_BASE["hgrn"]
                def proj_evac(w):
                    if w < 12 and w % 3:
                        return
                    dve.wait_ge(proj_read, w + 1)
                    p = w // 3 if w < 12 else w - 12
                    if w < 12 and p >= 2:
                        dve.wait_ge(chain_mm, STEP_AT[(p - 2, 7)] + 1)
                    if w >= 12:
                        ins = nc.vector.tensor_tensor(mix[:, 2 * p:2 * p + 2, :], mix[:, 2 * p:2 * p + 2, :],
                                                      sg_t[0][:, :, :], ALU.mult)
                    else:
                        ins = nc.vector.tensor_tensor(q_t[p % 2][:, :, :], sg_t[0][:, :, :], sg_t[1][:, :, :],
                                                      ALU.mult)
                    ins.then_inc(gates_used, 1)

                def make(p, s):
                    q, k, f = q_t[p % 2], k_t[p % 2], f_t[p % 2]
                    if s == "D":
                        dve.wait_ge(gates_used, p + 1)
                        dve.wait_ge(fk_ready, p + 1)
                        if p:
                            dve.wait_ge(chain_in, LEVELS * p)
                        step(nc.vector.memset(halves(r_t[:, :, :], 1)[1], 1.0))
                        return
                    h = 1 << s
                    _, fr = halves(f[:, :, :], h)
                    rl, _ = halves(r_t[:, :, :], h)
                    if s >= 3 or p:
                        before = STEP_AT[(p, s - 3)] if s >= 3 else STEP_AT[(p - 1, (6, 7, 5)[s])]
                        dve.wait_ge(chain_mm, before + 1)
                    dve.wait_ge(dve_link, link[0])
                    ins = nc.vector.tensor_tensor(
                        ql_view(s).rearrange("p a (n h) -> p a n h", h=h), halves(q[:, :, :], h)[1], fr, ALU.mult)
                    if s:
                        ins = nc.vector.tensor_tensor(halves(kl_t[s % 3][:, :, :], h)[0],
                                                      halves(k[:, :, :], h)[0], rl, ALU.mult)
                    ins.then_inc(chain_in, 1)
                    if s == 0:
                        step(nc.vector.tensor_copy(rl, fr))
                    elif s < LEVELS - 1:
                        shape = [P, 2, T // (2 * h), h]
                        step(nc.vector.tensor_tensor(rl, rl, fr[:, :, :, h - 1:h].broadcast_to(shape), ALU.mult))

                def double(p, s):
                    if s == "D" or s == LEVELS - 1:
                        return
                    h = 1 << s
                    fl, fr = halves(f_t[p % 2][:, :, :], h)
                    dve.wait_ge(dve_link, link[0])
                    step(nc.vector.tensor_tensor(fr, fr, fl[:, :, :, h - 1:h].broadcast_to([P, 2, T // (2 * h), h]),
                                                 ALU.mult))

                def take(c_, p, s):
                    if s == "O":
                        return
                    if s == "S":
                        dve.wait_ge(osd_ready, p + 1)
                        nc.vector.reciprocal(orstd[:, :], osd[:, :]).then_inc(orstd_ready, 1)
                        return
                    dve.wait_ge(chain_mm, c_ + 1)
                    if s == "B":
                        normed(c_, p)
                        return
                    bank = chain_bank(c_)
                    at = at_view(p)
                    if s == "D":
                        if p >= 2:
                            dve.wait_ge(chain_mm, STEP_AT[(p - 2, "O")] + 1)
                        eye = con[:, K_ID:K_ID + P].unsqueeze(1).broadcast_to([P, 4, P])
                        ins = nc.vector.tensor_tensor(at[:, :, 0, :],
                                                      bank.rearrange("p a (g t) -> p (a g) t", g=TG), eye, ALU.mult)
                    elif s == 7:
                        ins = nc.vector.tensor_copy(at[:, 0:4:2, 1, :],
                                                    bank[:, 0, :].rearrange("p (a t) -> p a t", a=2))
                    else:
                        h = 1 << s
                        n = 64 // h
                        dst = at[:, :, 0, :].rearrange("p q (n b h) -> p q n b h", b=2, h=h)[:, :, :, 1, :]
                        m = mask_t[:, s, :].rearrange("p (n h) -> p n h", h=h).unsqueeze(1)\
                            .broadcast_to([P, 4, n, h])
                        data = bank[:, 0, :].rearrange("p (q n h) -> p q n h", q=4, h=h)
                        dve.wait_ge(chain_read_dve, taken[0])
                        ins = nc.vector.copy_predicated(dst, m, data)
                    ins.then_inc(chain_read_dve, 1)
                    taken[0] += 1

                taken = [0]

                def normed(c_, p):
                    for hh in range(2):
                        j = 2 * p + hh
                        ins = nc.vector.scalar_tensor_tensor(out=mix[:, j, :], in0=o_t[:, hh, :],
                                                             scalar=vec[:, C_HGN + j:C_HGN + j + 1],
                                                             in1=chain_bank(c_)[:, hh, :], op0=ALU.mult, op1=ALU.mult)
                    ins.then_inc(o_normed, 1)

                def mix_rest(p):
                    dve.wait_ge(mix_hi, p + 1)
                    nc.vector.tensor_tensor(h_lo[:, 2 * p:2 * p + 2, :], mix[:, 2 * p:2 * p + 2, :],
                                            h_hi[:, 2 * p:2 * p + 2, :].bitcast(F32), ALU.subtract)\
                        .then_inc(mix_lo, 1)

                for b_ in range(3):
                    step(nc.vector.memset(kl_t[b_][:, :, :], 0.0))
                for w in range(19):
                    jobs = unit_jobs(u + w + 2) if w < 16 else []
                    takes = [x_ for x_ in enumerate(STEPS) if x_[1][0] == w - 1]
                    makes = [x_[1:] for x_ in STEPS if x_[0] == w and x_[2] not in ("O", "S", "B")]
                    if w == 16:
                        for p in range(NP_HG - 1):
                            mix_rest(p)
                    for i in range(max(len(jobs), len(takes), len(makes))):
                        if i < len(makes):
                            make(*makes[i])
                        if i < len(takes):
                            c_, (_, p, s) = takes[i]
                            take(c_, p, s)
                        if i < len(makes):
                            double(*makes[i])
                        if i < len(jobs):
                            split_lo(dve, *jobs[i])
                    if 1 <= w <= 12:
                        proj_evac(w - 1)
                    if 13 <= w <= 15 or w == 18:
                        p = w - 13 if w < 18 else 3
                        dve.wait_ge(o_normed, p + 1)
                        proj_evac(12 + p)
                    if w in HG_ADA:
                        one = ada_steps(ADA_HGRN + HG_ADA.index(w))
                        for k in range(KT):
                            one(k)
                    if w - 1 in HG_ADA:
                        ada_finish(ADA_HGRN + HG_ADA.index(w - 1))
                mix_rest(NP_HG - 1)
                for w in range(18, 20):
                    for j in unit_jobs(u + w):
                        split_lo(dve, *j)

            def swa():
                u = UNIT_BASE["swa"]

                def rope(r):
                    src = psum[4 + RING_AT[("C", r)] % 2][:, :].rearrange("p (a t) -> p a t", a=2) if r < 2 \
                        else raw_t[(r - 1) % 2]
                    dst = rk_t[r] if r < 2 else rq_t[r - 2]
                    cb = cosb[:, :].unsqueeze(1).broadcast_to([P, 2, T])
                    sb_ = sinb[:, :].unsqueeze(1).broadcast_to([P, 2, T])
                    dve.wait_ge(rope_mm, r + 1)
                    if r:
                        dve.wait_ge(rope_done, r)
                    nc.vector.tensor_tensor(rope_t[0][:, :, :], src[:, :, :], cb, ALU.mult)
                    linked(nc.vector.tensor_tensor(
                        rope_t[1][:, :, :], psum[r_bank(r)][:, :].rearrange("p (a t) -> p a t", a=2), sb_, ALU.mult))
                    if r < 2:
                        ins = nc.vector.tensor_tensor(dst[:, :, :], rope_t[0][:, :, :], rope_t[1][:, :, :], ALU.add)
                    else:
                        by_chunk = dst[:, :, :].rearrange("p a t -> p (a t)")\
                            .rearrange("p (n a c) -> p a n c", a=2, c=CH)
                        ins = nc.vector.tensor_tensor(
                            by_chunk, rope_t[0][:, :, :].rearrange("p a (n c) -> p a n c", c=CH),
                            rope_t[1][:, :, :].rearrange("p a (n c) -> p a n c", c=CH), ALU.add)
                    ins.then_inc(rope_done, 1)

                def evac_v():
                    dve.wait_ge(w_used, 2 * (u + 2))
                    nc.vector.tensor_tensor(
                        vt_t[:, :, :], psum[2][:, :].rearrange("p (a t) -> p a t", a=2),
                        bv[:, :].unsqueeze(1).broadcast_to([P, 2, T]), ALU.add).then_inc(sw_v, 1)
                    dve.wait_ge(sw_v, 1)
                    nc.vector.tensor_copy(vmix_t[0:64, 0, :], vt_t[0:64, 1, :])
                    nc.vector.tensor_copy(vmix_t[64:P, 0, :], vt_t[64:P, 0, :]).then_inc(sw_v, 1)

                def bound(b):
                    jh, n = b // 4, b % 4
                    keys = CH if n == 0 else 2 * CH
                    st = stat[:, b % 2, :, :]
                    dve.wait_ge(s_mm, b + 1)
                    if b >= 2:
                        dve.wait_ge(p_exp, 5 * (b - 1))
                    snk = sink[:, 4 * jh:4 * jh + 4]
                    linked(nc.vector.tensor_reduce(
                        st[:, 0, :], psum[s_bank(b)][:, :].rearrange("p (j t) -> p j t", j=4)[:, :, 0:keys], AX,
                        ALU.max))
                    linked(nc.vector.scalar_tensor_tensor(out=st[:, 1, :], in0=st[:, 0, :], scalar=0.125, in1=snk,
                                                          op0=ALU.mult, op1=ALU.max))
                    nc.vector.tensor_scalar(st[:, 2, :], st[:, 1, :], -1.0, None, ALU.mult)
                    nc.vector.tensor_tensor(st[:, 3, :], snk, st[:, 1, :], ALU.subtract).then_inc(s_max, 1)

                def norm(b):
                    keys = CH if b % 4 == 0 else 2 * CH
                    st = stat[:, b % 2, :, :]
                    dve.wait_ge(p_exp, 5 * (b + 1))
                    linked(nc.vector.tensor_tensor(st[:, 6, :], st[:, 4, :], st[:, 5, :], ALU.add))
                    linked(nc.vector.reciprocal(st[:, 7, :], st[:, 6, :]))
                    blk = p_block(b)[:, :, 0:keys]
                    nc.vector.tensor_tensor(blk, blk, st[:, 7, :].unsqueeze(2).broadcast_to([P, 4, keys]), ALU.mult)\
                        .then_inc(p_norm, 1)

                def split_unit(w):
                    for j in unit_jobs(u + w):
                        split_lo(dve, *j)

                for w in range(4):
                    if w == 1:
                        rope(0)
                        evac_v()
                    split_unit(w + 2)
                    if w == 1:
                        rope(1)
                    one = ada_steps(ADA_SWA + w)
                    for k in range(KT):
                        one(k)
                    if w:
                        ada_finish(ADA_SWA + w - 1)
                    if w == 2:
                        rope(2)
                split_unit(6)
                rope(3)
                split_unit(7)
                ada_finish(ADA_SWA + 3)
                bound(0)
                norm(0)
                bound(1)
                rope(4)
                norm(1)
                bound(2)
                rope(5)
                for b in range(3, 9):
                    norm(b - 1)
                    if b < 8:
                        bound(b)
                    if b == 6:
                        for jp in range(2):
                            o_lo(jp)
                for jp in range(2, 4):
                    o_lo(jp)
                split_unit(8)
                split_unit(9)

            def o_lo(jp):
                dve.wait_ge(mix_hi, 4 + jp + 1)
                nc.vector.tensor_tensor(h_lo[:, 2 * jp:2 * jp + 2, :], psum[jp][:, :].rearrange("p (a t) -> p a t", a=2),
                                        h_hi[:, 2 * jp:2 * jp + 2, :].bitcast(F32), ALU.subtract).then_inc(mix_lo, 1)

            stage_part(0)
            ffn(0)
            dve.wait_ge(c_ready, 2)
            linked(nc.vector.tensor_tensor(small[:, 3, :], small[:, 0, :], small[:, 1, :], ALU.add))
            linked(nc.vector.tensor_tensor(small[:, 3, :], small[:, 3, :], small[:, 2, :], ALU.add))
            linked(nc.vector.reciprocal(small[:, 4, :], small[:, 3, :]))
            linked(nc.vector.tensor_tensor(lb[:, :], small[:, 0, :], small[:, 4, :], ALU.mult))
            nc.vector.tensor_scalar(oml[:, :], lb[:, :], -1.0, 1.0, ALU.mult, ALU.add).then_inc(lb_ready, 1)
            dve.wait_ge(c_ready, 4)
            stage_part(1)
            hgrn()
            stage_part(2)
            ffn(1)
            stage_part(3)
            ffn(2)
            stage_part(4)
            swa()
            stage_part(5)
            ffn(3)
            stage_part(6)


_INS = ["x", "c", "positions", "ada_w", "ada_b", "norm_g", "ffn1_w_gu", "ffn1_w_down", "ffn2_w_gu", "ffn2_w_down",
        "hg_w_in", "hg_lower_bounds", "hg_norm_g", "hg_w_out", "sw_w_qkv", "sw_b_qkv", "sw_sinks", "sw_w_out",
        "sw_b_out", "final_norm_g"]


def kernel(**inputs):
    import concourse.bacc as _bacc
    from concourse import mybir as _mybir
    from concourse.bass_utils import run_bass_kernel_spmd as _run

    nc = _bacc.Bacc("TRN2", target_bir_lowering=False, num_devices=1)
    arrays, args = {}, []
    for name, a in [(n, inputs[n]) for n in _INS] + list(zip(("consts", "masks"), constants())):
        a = np.ascontiguousarray(a)
        arrays[f"in_{name}_dram"] = a
        args.append(nc.dram_tensor(f"in_{name}_dram", a.shape, _mybir.dt.from_np(a.dtype), kind="ExternalInput").ap())
    out = nc.dram_tensor("out_dram", (1, T, D), _mybir.dt.float32, kind="ExternalOutput").ap()
    trunk(nc, *args, out)
    r = _run(nc, [arrays], core_ids=[0])
    return r.results[0]["out_dram"]
```
